# Optimizing a Trainium2 kernel written in Bass

```python
import math
import jax, jax.numpy as jnp
from jax import lax
import numpy as np
import jax
import jax.numpy as jnp

D_MODEL = 1024
BATCH = 1
SEQ = 256
DEPTH = 2

GRID_W = 64
CTX_LEN = 256

MLA_HEADS = 8
QK_NOPE = 64
QK_ROPE = 32
V_HEAD = 64
Q_LORA = 384
KV_LORA = 256
AXIS_ROPE = QK_ROPE // 2
ROPE_BASE = 10000.0
Q_BLOCK = 128

FNET_GROUPS = 4
FNET_GROUP_W = 64
FNET_W = FNET_GROUPS * FNET_GROUP_W

HYENA_W = 256
HYENA_CONV = 3
FILTER_EMB = 33
FILTER_ORDER = 64
DECAY_TARGET = 1e-2
FAST_DECAY_PCT = 0.3
SLOW_DECAY_PCT = 1.5

MLA_W = MLA_HEADS * V_HEAD
MIX_W = MLA_W + FNET_W + HYENA_W
OFF_Q = 0
OFF_KV = OFF_Q + Q_LORA
OFF_KR = OFF_KV + KV_LORA
OFF_F = OFF_KR + QK_ROPE
OFF_H = OFF_F + FNET_W
IN_W = OFF_H + 3 * HYENA_W
D_FF = 4 * D_MODEL
N_MOD = 6
EPS = 1e-6


def rms_norm(x, g):
    xf = x.astype(jnp.float32)
    y = xf * lax.rsqrt(jnp.mean(xf * xf, axis=-1, keepdims=True) + EPS)
    return (y * g.astype(jnp.float32)).astype(x.dtype)

def modulation(cvec, w_mod, b_mod):
    m = (jax.nn.silu(cvec) @ w_mod + b_mod).reshape(-1, 1, N_MOD * D_MODEL)
    return jnp.split(m, N_MOD, axis=-1)

def modulate(h, shift, scale):
    return h * (1.0 + scale) + shift

def grid_rope_tables(n_tokens, dtype):
    rows = n_tokens // GRID_W
    row = jnp.repeat(jnp.arange(rows, dtype=jnp.float32), GRID_W)
    col = jnp.tile(jnp.arange(GRID_W, dtype=jnp.float32), rows)
    inv = ROPE_BASE ** (-jnp.arange(0, AXIS_ROPE, 2, dtype=jnp.float32) / AXIS_ROPE)
    ang = jnp.concatenate([row[:, None] * inv, col[:, None] * inv], axis=-1)
    return jnp.cos(ang).astype(dtype), jnp.sin(ang).astype(dtype)

def _rotate_half(v, cos, sin):
    half = v.shape[-1] // 2
    v1, v2 = v[..., :half], v[..., half:]
    return jnp.concatenate([v1 * cos - v2 * sin, v1 * sin + v2 * cos], axis=-1)

def apply_axial_rope(x, cos, sin):
    n = AXIS_ROPE // 2
    return jnp.concatenate([
        _rotate_half(x[..., :AXIS_ROPE], cos[..., :n], sin[..., :n]),
        _rotate_half(x[..., AXIS_ROPE:], cos[..., n:], sin[..., n:])], axis=-1)

def mla_queries(p, q_norm_g, w_uq, rope):
    B, L, _ = p.shape
    cq = rms_norm(p[..., OFF_Q:OFF_KV], q_norm_g)
    q = (cq @ w_uq).reshape(B, L, MLA_HEADS, QK_NOPE + QK_ROPE)
    q_nope, q_rope = q[..., :QK_NOPE], q[..., QK_NOPE:]
    if rope is not None:
        cos, sin = rope
        q_rope = apply_axial_rope(q_rope, cos[:, None, :], sin[:, None, :])
    return q_nope, q_rope

def mla_keys_values(p_kv, kv_norm_g, w_ukv, rope):
    B, L, _ = p_kv.shape
    ckv = rms_norm(p_kv[..., :KV_LORA], kv_norm_g)
    kv = (ckv @ w_ukv).reshape(B, L, MLA_HEADS, QK_NOPE + V_HEAD)
    k_rope = p_kv[..., KV_LORA:]
    if rope is not None:
        k_rope = apply_axial_rope(k_rope, *rope)
    return kv[..., :QK_NOPE], k_rope, kv[..., QK_NOPE:]

def mla_attention(q_nope, q_rope, k_nope, k_rope, v):
    B, L, H, _ = q_nope.shape
    nb = L // Q_BLOCK
    scale = 1.0 / math.sqrt(QK_NOPE + QK_ROPE)

    def to_blocks(t):
        return jnp.moveaxis(t.reshape(B, nb, Q_BLOCK, *t.shape[2:]), 1, 0)

    def block(qs):
        qn, qr = qs
        s = (jnp.einsum('bqhd,bkhd->bhqk', qn, k_nope)
             + jnp.einsum('bqhr,bkr->bhqk', qr, k_rope))
        prob = jax.nn.softmax(s.astype(jnp.float32) * scale, axis=-1).astype(v.dtype)
        return jnp.einsum('bhqk,bkhd->bqhd', prob, v)

    o = lax.map(block, (to_blocks(q_nope), to_blocks(q_rope)))
    return jnp.moveaxis(o, 0, 1).reshape(B, L, H * V_HEAD)

def fourier_mix(u):
    B, L, _ = u.shape
    g = u.reshape(B, L, FNET_GROUPS, FNET_GROUP_W).astype(jnp.float32)
    f = jnp.fft.fftn(g, axes=(1, 3), norm="ortho").real
    return f.reshape(B, L, FNET_W).astype(u.dtype)

def short_conv(u, w, b):
    L = u.shape[1]
    pad = (HYENA_CONV - 1) // 2
    up = jnp.pad(u, ((0, 0), (pad, HYENA_CONV - 1 - pad), (0, 0)))
    out = b
    for k in range(HYENA_CONV):
        out = out + up[:, k:k + L] * w[k]
    return out

def hyena_filters(L, w1, b1, freq, w2, b2, w3):
    f32 = jnp.float32
    t = jnp.linspace(0.0, 1.0, L, dtype=f32)[:, None]
    bands = (FILTER_EMB - 1) // 2
    fr = jnp.linspace(1e-4, bands - 1, bands, dtype=f32)
    ang = 2.0 * math.pi * jnp.arange(L, dtype=f32)[:, None] / L * fr
    z = jnp.concatenate([t, jnp.cos(ang), -jnp.sin(ang)], axis=-1)
    h = jnp.sin(freq * (z.astype(w1.dtype) @ w1 + b1))
    h = jnp.sin(freq * (h @ w2 + b2))
    h = (h @ w3).astype(f32)
    min_decay = math.log(DECAY_TARGET) / SLOW_DECAY_PCT
    max_decay = math.log(DECAY_TARGET) / FAST_DECAY_PCT
    deltas = jnp.abs(jnp.linspace(min_decay, max_decay, HYENA_W, dtype=f32))
    decay = jnp.exp(-t * deltas)
    h = h * jnp.tile(decay, (1, 2))
    h_fwd, h_bwd = h[:, :HYENA_W], h[:, HYENA_W:]
    k = jnp.concatenate([h_fwd, jnp.zeros((1, HYENA_W), f32), h_bwd[:0:-1]], axis=0)
    return k / jnp.sum(jnp.abs(k), axis=0, keepdims=True)

def hyena_mix(u, conv_w, conv_b, w1, b1, freq, w2, b2, w3, d_bias):
    B, L, _ = u.shape
    u = short_conv(u, conv_w, conv_b)
    x0, x1, v = jnp.split(u, 3, axis=-1)
    z = (x1 * v).astype(jnp.float32)
    k = hyena_filters(L, w1, b1, freq, w2, b2, w3)
    zf = jnp.fft.rfft(z, n=2 * L, axis=1)
    kf = jnp.fft.rfft(k, n=2 * L, axis=0)
    y = jnp.fft.irfft(zf * kf[None], n=2 * L, axis=1)[:, :L] + d_bias.astype(jnp.float32) * z
    return (x0.astype(jnp.float32) * y).astype(u.dtype)

def heads_out(att, p, hy, w_out):
    f = fourier_mix(p[..., OFF_F:OFF_H])
    hz = hyena_mix(p[..., OFF_H:], *hy)
    return jnp.concatenate([att, f, hz], axis=-1) @ w_out

def sq_relu_mlp(h, w1, w2):
    return jnp.square(jax.nn.relu(h @ w1)) @ w2

def first_inputs(seed: int = 0) -> dict:
    key = jax.random.key(seed)
    ks = jax.random.split(key, 26)

    def nrm(k, shape, scale):
        return jax.random.normal(k, shape, jnp.float32) * scale

    D = D_MODEL
    return {
        "x": nrm(ks[0], (BATCH, SEQ, D), 1.0),
        "c": nrm(ks[1], (BATCH, D), 1.0),
        "ctx": nrm(ks[2], (BATCH, CTX_LEN, D), 1.0),
        "c_ctx": nrm(ks[3], (D,), 1.0),
        "norm1_g": 1.0 + nrm(ks[4], (DEPTH, D), 0.05),
        "norm2_g": 1.0 + nrm(ks[5], (DEPTH, D), 0.05),
        "w_mod": nrm(ks[6], (DEPTH, D, N_MOD * D), 0.5 * D ** -0.5),
        "b_mod": nrm(ks[7], (DEPTH, N_MOD * D), 0.01),
        "w_in": nrm(ks[8], (DEPTH, D, IN_W), D ** -0.5),
        "q_norm_g": 1.0 + nrm(ks[9], (DEPTH, Q_LORA), 0.05),
        "kv_norm_g": 1.0 + nrm(ks[10], (DEPTH, KV_LORA), 0.05),
        "w_uq": nrm(ks[11], (DEPTH, Q_LORA, MLA_HEADS * (QK_NOPE + QK_ROPE)), Q_LORA ** -0.5),
        "w_ukv": nrm(ks[12], (DEPTH, KV_LORA, MLA_HEADS * (QK_NOPE + V_HEAD)), KV_LORA ** -0.5),
        "hy_conv_w": nrm(ks[13], (DEPTH, HYENA_CONV, 3 * HYENA_W), HYENA_CONV ** -0.5),
        "hy_conv_b": nrm(ks[14], (DEPTH, 3 * HYENA_W), 0.01),
        "hy_w1": nrm(ks[15], (DEPTH, FILTER_EMB, FILTER_ORDER), FILTER_EMB ** -0.5),
        "hy_b1": nrm(ks[16], (DEPTH, FILTER_ORDER), 0.1),
        "hy_freq": 1.0 + nrm(ks[17], (DEPTH, FILTER_ORDER), 0.05),
        "hy_w2": nrm(ks[18], (DEPTH, FILTER_ORDER, FILTER_ORDER), FILTER_ORDER ** -0.5),
        "hy_b2": nrm(ks[19], (DEPTH, FILTER_ORDER), 0.1),
        "hy_w3": nrm(ks[20], (DEPTH, FILTER_ORDER, 2 * HYENA_W), FILTER_ORDER ** -0.5),
        "hy_d": nrm(ks[21], (DEPTH, HYENA_W), 0.5),
        "w_out": nrm(ks[22], (DEPTH, MIX_W, D), MIX_W ** -0.5),
        "w_mlp1": nrm(ks[23], (DEPTH, D, D_FF), D ** -0.5),
        "w_mlp2": nrm(ks[24], (DEPTH, D_FF, D), D_FF ** -0.5),
        "final_norm_g": 1.0 + nrm(ks[25], (D,), 0.05),
    }

def first_block(x, c, ctx, c_ctx, norm1_g, norm2_g, w_mod, b_mod, w_in, q_norm_g, kv_norm_g,
              w_uq, w_ukv, hy_conv_w, hy_conv_b, hy_w1, hy_b1, hy_freq, hy_w2, hy_b2, hy_w3,
              hy_d, w_out, w_mlp1, w_mlp2, final_norm_g):
    L = x.shape[1]
    rope = grid_rope_tables(L, x.dtype)
    xc = ctx
    for l in range(DEPTH):
        last = l == DEPTH - 1
        hy = (hy_conv_w[l], hy_conv_b[l], hy_w1[l], hy_b1[l], hy_freq[l],
              hy_w2[l], hy_b2[l], hy_w3[l], hy_d[l])
        sh1, sc1, g1, sh2, sc2, g2 = modulation(c, w_mod[l], b_mod[l])
        csh1, csc1, cg1, csh2, csc2, cg2 = modulation(c_ctx, w_mod[l], b_mod[l])

        hx = modulate(rms_norm(x, norm1_g[l]), sh1, sc1)
        hc = modulate(rms_norm(xc, norm1_g[l]), csh1, csc1)
        px = hx @ w_in[l]
        if last:
            pc_kv = hc @ w_in[l][:, OFF_KV:OFF_F]
        else:
            pc = hc @ w_in[l]
            pc_kv = pc[..., OFF_KV:OFF_F]
        kn_c, kr_c, v_c = mla_keys_values(pc_kv, kv_norm_g[l], w_ukv[l], None)
        kn_x, kr_x, v_x = mla_keys_values(px[..., OFF_KV:OFF_F], kv_norm_g[l], w_ukv[l], rope)
        qn_x, qr_x = mla_queries(px, q_norm_g[l], w_uq[l], rope)
        att_x = mla_attention(qn_x, qr_x,
                              jnp.concatenate([kn_x, kn_c], axis=1),
                              jnp.concatenate([kr_x, kr_c], axis=1),
                              jnp.concatenate([v_x, v_c], axis=1))
        x = x + g1 * heads_out(att_x, px, hy, w_out[l])

        x = x + g2 * sq_relu_mlp(modulate(rms_norm(x, norm2_g[l]), sh2, sc2), w_mlp1[l], w_mlp2[l])

        if not last:
            qn_c, qr_c = mla_queries(pc, q_norm_g[l], w_uq[l], None)
            att_c = mla_attention(qn_c, qr_c, kn_c, kr_c, v_c)
            xc = xc + cg1 * heads_out(att_c, pc, hy, w_out[l])
            xc = xc + cg2 * sq_relu_mlp(modulate(rms_norm(xc, norm2_g[l]), csh2, csc2),
                                        w_mlp1[l], w_mlp2[l])
    return rms_norm(x, final_norm_g)


N_MIXERS = 3
D_FF_2 = 4 * D_MODEL
NORM_EPS = 1e-6

DN_K_HEADS = 8
DN_V_HEADS = 16
DN_HEAD_K = 128
DN_HEAD_V = 128
DN_GROUP = DN_V_HEADS // DN_K_HEADS
DN_K_DIM = DN_K_HEADS * DN_HEAD_K
DN_V_DIM = DN_V_HEADS * DN_HEAD_V
DN_QKV_DIM = 2 * DN_K_DIM + DN_V_DIM
DN_IN_DIM = DN_QKV_DIM + DN_V_DIM + 4 * DN_V_HEADS
SHORT_CONV = 5
DN_CHUNK = 64

GLA_HEADS = 4
GLA_K_DIM = D_MODEL // 2
GLA_V_DIM = D_MODEL
GLA_HEAD_K = GLA_K_DIM // GLA_HEADS
GLA_HEAD_V = GLA_V_DIM // GLA_HEADS
GLA_GATE_RANK = 16
GLA_GATE_NORMALIZER = 16.0
GLA_IN_DIM = 2 * GLA_K_DIM + 2 * GLA_V_DIM + 2 * GLA_GATE_RANK
GLA_CHUNK = 64

ATTN_Q_HEADS = 8
ATTN_KV_HEADS = 2
ATTN_HEAD_DIM = 128
ATTN_GROUP = ATTN_Q_HEADS // ATTN_KV_HEADS
ATTN_Q_DIM = ATTN_Q_HEADS * ATTN_HEAD_DIM
ATTN_KV_DIM = ATTN_KV_HEADS * ATTN_HEAD_DIM
ATTN_IN_DIM = ATTN_Q_DIM + 2 * ATTN_KV_DIM
ROPE_THETA = 10000.0


F32 = jnp.float32

def rms_norm_2(x, g):
    xf = x.astype(F32)
    y = xf * lax.rsqrt(jnp.mean(xf * xf, axis=-1, keepdims=True) + NORM_EPS)
    return (y * g.astype(F32)).astype(x.dtype)

def l2_normalize(x):
    xf = x.astype(F32)
    return xf * lax.rsqrt(jnp.sum(xf * xf, axis=-1, keepdims=True) + NORM_EPS)

def modulate_2(h, shift, scale):
    return h * (1.0 + scale) + shift

def squared_relu_ffn(h, w1, w2):
    return jnp.square(jax.nn.relu(h @ w1)) @ w2

def short_conv_2(u, w):
    n = u.shape[1]
    pad = SHORT_CONV // 2
    up = jnp.pad(u, ((0, 0), (pad, pad), (0, 0)))
    out = up[:, 0:n] * w[:, 0]
    for tap in range(1, SHORT_CONV):
        out = out + up[:, tap:tap + n] * w[:, tap]
    return out

def to_chunks(t, chunk):
    b, h, n = t.shape[:3]
    t = t.reshape((b, h, n // chunk, chunk) + t.shape[3:])
    return jnp.moveaxis(t, 2, 0)

def from_chunks(t):
    t = jnp.moveaxis(t, 0, 2)
    b, h, nc, chunk = t.shape[:4]
    return t.reshape((b, h, nc * chunk) + t.shape[4:])

def time_flip(t):
    return jnp.flip(t, axis=2)

def identity(t):
    return t

def axial_rope_tables(n_rows):
    row = jnp.repeat(jnp.arange(n_rows), GRID_W).astype(F32)
    col = jnp.tile(jnp.arange(GRID_W), n_rows).astype(F32)
    axis_dim = ATTN_HEAD_DIM // 2
    inv_freq = jnp.power(ROPE_THETA, -jnp.arange(0, axis_dim, 2, dtype=F32) / axis_dim)
    ang_row = row[:, None] * inv_freq
    ang_col = col[:, None] * inv_freq
    return jnp.cos(ang_row), jnp.sin(ang_row), jnp.cos(ang_col), jnp.sin(ang_col)

def rotate_pairs(x, cos, sin):
    x1, x2 = jnp.split(x, 2, axis=-1)
    cs, sn = cos[:, None, :], sin[:, None, :]
    return jnp.concatenate([x1 * cs - x2 * sn, x1 * sn + x2 * cs], axis=-1)

def apply_axial_rope_2(x, tables):
    cos_r, sin_r, cos_c, sin_c = tables
    xf = x.astype(F32)
    half = ATTN_HEAD_DIM // 2
    y = jnp.concatenate([rotate_pairs(xf[..., :half], cos_r, sin_r),
                         rotate_pairs(xf[..., half:], cos_c, sin_c)], axis=-1)
    return y.astype(x.dtype)

def gated_delta_rule(q, k, v, g, beta, state):
    c = DN_CHUNK
    tri = jnp.tril(jnp.ones((c, c), dtype=bool))
    strict = jnp.tril(jnp.ones((c, c), dtype=bool), -1)
    eye = jnp.eye(c, dtype=F32)

    def step(s, xs):
        qc, kc, vc, gc, bc = xs
        qc = jnp.repeat(qc, DN_GROUP, axis=1)
        kc = jnp.repeat(kc, DN_GROUP, axis=1)
        gcum = jnp.cumsum(gc, axis=-1)
        decay = jnp.exp(jnp.where(tri, gcum[..., :, None] - gcum[..., None, :], -jnp.inf))
        kk = jnp.einsum('bhid,bhjd->bhij', kc, kc)
        m = jnp.where(strict, bc[..., :, None] * kk * decay, 0.0)
        rhs = jnp.concatenate([vc * bc[..., None], kc * (bc * jnp.exp(gcum))[..., None]], axis=-1)
        sol = lax.linalg.triangular_solve(eye + m, rhs, left_side=True, lower=True, unit_diagonal=True)
        u, w = sol[..., :DN_HEAD_V], sol[..., DN_HEAD_V:]
        v_new = u - jnp.einsum('bhid,bhdv->bhiv', w, s)
        a_qk = jnp.einsum('bhid,bhjd->bhij', qc, kc) * decay
        o = (jnp.einsum('bhid,bhdv->bhiv', qc * jnp.exp(gcum)[..., None], s)
             + jnp.einsum('bhij,bhjv->bhiv', a_qk, v_new))
        tail = jnp.exp(gcum[..., -1:] - gcum)
        s = (s * jnp.exp(gcum[..., -1])[..., None, None]
             + jnp.einsum('bhjd,bhjv->bhdv', kc * tail[..., None], v_new))
        return s, o

    xs = (to_chunks(q, c), to_chunks(k, c), to_chunks(v, c), to_chunks(g, c), to_chunks(beta, c))
    state, o = lax.scan(step, state, xs)
    return from_chunks(o), state

def gla_rule(q, k, v, gk, state):
    c = GLA_CHUNK
    tri = jnp.tril(jnp.ones((c, c), dtype=bool))[:, :, None]

    def step(s, xs):
        qc, kc, vc, gc = xs
        bcum = jnp.cumsum(gc, axis=-2)
        rel = jnp.exp(jnp.where(tri, bcum[..., :, None, :] - bcum[..., None, :, :], -jnp.inf))
        a_qk = jnp.einsum('bhid,bhjd,bhijd->bhij', qc, kc, rel)
        o = (jnp.einsum('bhij,bhjv->bhiv', a_qk, vc)
             + jnp.einsum('bhid,bhdv->bhiv', qc * jnp.exp(bcum), s))
        last = bcum[..., -1:, :]
        s = (s * jnp.exp(last[..., 0, :])[..., None]
             + jnp.einsum('bhjd,bhjv->bhdv', kc * jnp.exp(last - bcum), vc))
        return s, o

    xs = (to_chunks(q, c), to_chunks(k, c), to_chunks(v, c), to_chunks(gk, c))
    state, o = lax.scan(step, state, xs)
    return from_chunks(o), state

def deltanet_mixer(hx, hc, w_in, conv_w, a_log, dt_bias, norm_g, w_out, with_ctx_out):
    def project(h):
        bsz, n, _ = h.shape
        p = h @ w_in
        qkv = jax.nn.silu(short_conv_2(p[..., :DN_QKV_DIM], conv_w))
        z = p[..., DN_QKV_DIM:DN_QKV_DIM + DN_V_DIM]
        ab = p[..., DN_QKV_DIM + DN_V_DIM:].astype(F32)
        q = l2_normalize(qkv[..., :DN_K_DIM].reshape(bsz, n, DN_K_HEADS, DN_HEAD_K)) * DN_HEAD_K ** -0.5
        k = l2_normalize(qkv[..., DN_K_DIM:2 * DN_K_DIM].reshape(bsz, n, DN_K_HEADS, DN_HEAD_K))
        v = qkv[..., 2 * DN_K_DIM:].reshape(bsz, n, DN_V_HEADS, DN_HEAD_V).astype(F32)
        a = ab[..., :2 * DN_V_HEADS].reshape(bsz, n, 2, DN_V_HEADS)
        b = ab[..., 2 * DN_V_HEADS:].reshape(bsz, n, 2, DN_V_HEADS)
        g = -jnp.exp(a_log.astype(F32)) * jax.nn.softplus(a + dt_bias.astype(F32))
        beta = jax.nn.sigmoid(b)
        return (jnp.swapaxes(q, 1, 2), jnp.swapaxes(k, 1, 2), jnp.swapaxes(v, 1, 2),
                jnp.moveaxis(g, 1, -1), jnp.moveaxis(beta, 1, -1), z)

    qx, kx, vx, gx, bx, zx = project(hx)
    qc, kc, vc, gc, bc, zc = project(hc)
    bsz = hx.shape[0]
    out_x, out_c = [], []
    for d in range(2):
        flip = time_flip if d == 1 else identity
        state0 = jnp.zeros((bsz, DN_V_HEADS, DN_HEAD_K, DN_HEAD_V), F32)
        oc, state_c = gated_delta_rule(flip(qc), flip(kc), flip(vc), flip(gc[:, d]), flip(bc[:, d]), state0)
        ox, _ = gated_delta_rule(flip(qx), flip(kx), flip(vx), flip(gx[:, d]), flip(bx[:, d]), state_c)
        out_x.append(flip(ox))
        out_c.append(flip(oc))

    def readout(o, z):
        bsz_, n = z.shape[:2]
        o = rms_norm_2(jnp.swapaxes(o, 1, 2), norm_g)
        o = o * jax.nn.silu(z.reshape(bsz_, n, DN_V_HEADS, DN_HEAD_V).astype(F32))
        return o.reshape(bsz_, n, DN_V_DIM).astype(z.dtype) @ w_out

    yx = readout(out_x[0] + out_x[1], zx)
    yc = readout(out_c[0] + out_c[1], zc) if with_ctx_out else None
    return yx, yc

def gla_mixer(hx, hc, w_in, gate_w2, gate_b2, norm_g, w_out, with_ctx_out):
    def project(h):
        bsz, n, _ = h.shape
        p = h @ w_in
        q = p[..., :GLA_K_DIM].reshape(bsz, n, GLA_HEADS, GLA_HEAD_K).astype(F32) * GLA_HEAD_K ** -0.5
        k = p[..., GLA_K_DIM:2 * GLA_K_DIM].reshape(bsz, n, GLA_HEADS, GLA_HEAD_K).astype(F32)
        v = p[..., 2 * GLA_K_DIM:2 * GLA_K_DIM + GLA_V_DIM].reshape(bsz, n, GLA_HEADS, GLA_HEAD_V).astype(F32)
        gate = p[..., 2 * GLA_K_DIM + GLA_V_DIM:2 * GLA_K_DIM + 2 * GLA_V_DIM]
        low = p[..., 2 * GLA_K_DIM + 2 * GLA_V_DIM:].reshape(bsz, n, 2, GLA_GATE_RANK)
        logits = jnp.einsum('btdr,drk->btdk', low, gate_w2) + gate_b2
        gk = jax.nn.log_sigmoid(logits.astype(F32)) / GLA_GATE_NORMALIZER
        gk = gk.reshape(bsz, n, 2, GLA_HEADS, GLA_HEAD_K).transpose(0, 2, 3, 1, 4)
        return jnp.swapaxes(q, 1, 2), jnp.swapaxes(k, 1, 2), jnp.swapaxes(v, 1, 2), gk, gate

    qx, kx, vx, gx, zx = project(hx)
    qc, kc, vc, gc, zc = project(hc)
    bsz = hx.shape[0]
    out_x, out_c = [], []
    for d in range(2):
        flip = time_flip if d == 1 else identity
        state0 = jnp.zeros((bsz, GLA_HEADS, GLA_HEAD_K, GLA_HEAD_V), F32)
        oc, state_c = gla_rule(flip(qc), flip(kc), flip(vc), flip(gc[:, d]), state0)
        ox, _ = gla_rule(flip(qx), flip(kx), flip(vx), flip(gx[:, d]), state_c)
        out_x.append(flip(ox))
        out_c.append(flip(oc))

    def readout(o, z):
        bsz_, n = z.shape[:2]
        o = rms_norm_2(jnp.swapaxes(o, 1, 2), norm_g)
        o = o * jax.nn.silu(z.reshape(bsz_, n, GLA_HEADS, GLA_HEAD_V).astype(F32))
        return o.reshape(bsz_, n, GLA_V_DIM).astype(z.dtype) @ w_out

    yx = readout(out_x[0] + out_x[1], zx)
    yc = readout(out_c[0] + out_c[1], zc) if with_ctx_out else None
    return yx, yc

def attention_mixer(hx, hc, w_in, q_norm_g, k_norm_g, w_out, rope, with_ctx_out):
    def project(h):
        bsz, n, _ = h.shape
        p = h @ w_in
        q = p[..., :ATTN_Q_DIM].reshape(bsz, n, ATTN_Q_HEADS, ATTN_HEAD_DIM)
        k = p[..., ATTN_Q_DIM:ATTN_Q_DIM + ATTN_KV_DIM].reshape(bsz, n, ATTN_KV_HEADS, ATTN_HEAD_DIM)
        v = p[..., ATTN_Q_DIM + ATTN_KV_DIM:].reshape(bsz, n, ATTN_KV_HEADS, ATTN_HEAD_DIM)
        return rms_norm_2(q, q_norm_g), rms_norm_2(k, k_norm_g), v

    qx, kx, vx = project(hx)
    qc, kc, vc = project(hc)
    qx = apply_axial_rope_2(qx, rope)
    kx = apply_axial_rope_2(kx, rope)
    bsz, n = hx.shape[:2]
    scale = ATTN_HEAD_DIM ** -0.5

    def attend(q_blk, keys, values):
        s = jnp.einsum('bkgqd,bksd->bkgqs', q_blk, keys).astype(F32) * scale
        p = jax.nn.softmax(s, axis=-1).astype(values.dtype)
        return jnp.einsum('bkgqs,bksd->bkgqd', p, values)

    k_all = jnp.concatenate([kx, kc], axis=1).transpose(0, 2, 1, 3)
    v_all = jnp.concatenate([vx, vc], axis=1).transpose(0, 2, 1, 3)
    n_blk = n // Q_BLOCK
    q_blocks = qx.reshape(bsz, n_blk, Q_BLOCK, ATTN_KV_HEADS, ATTN_GROUP, ATTN_HEAD_DIM).transpose(1, 0, 3, 4, 2, 5)
    o = lax.map(lambda qb: attend(qb, k_all, v_all), q_blocks)
    yx = o.transpose(1, 0, 4, 2, 3, 5).reshape(bsz, n, ATTN_Q_DIM) @ w_out
    yc = None
    if with_ctx_out:
        lc = hc.shape[1]
        q_ctx = qc.reshape(bsz, lc, ATTN_KV_HEADS, ATTN_GROUP, ATTN_HEAD_DIM).transpose(0, 2, 3, 1, 4)
        oc = attend(q_ctx, kc.transpose(0, 2, 1, 3), vc.transpose(0, 2, 1, 3))
        yc = oc.transpose(0, 3, 1, 2, 4).reshape(bsz, lc, ATTN_Q_DIM) @ w_out
    return yx, yc

def second_inputs(seed: int = 0) -> dict:
    key = jax.random.key(seed)
    ks = jax.random.split(key, 32)
    n_a = len(range(0, DEPTH, N_MIXERS))
    n_b = len(range(1, DEPTH, N_MIXERS))
    n_c = len(range(2, DEPTH, N_MIXERS))

    def normal(k, shape, scale):
        return jax.random.normal(k, shape, F32) * scale

    def gain(k, shape):
        return 1.0 + normal(k, shape, 0.02)

    dt = jnp.exp(jax.random.uniform(ks[12], (n_a, 2, DN_V_HEADS), F32, math.log(1e-3), math.log(1e-1)))
    return {
        'x': normal(ks[0], (BATCH, SEQ, D_MODEL), 1.0),
        'c': normal(ks[1], (BATCH, D_MODEL), 1.0),
        'ctx': normal(ks[2], (BATCH, CTX_LEN, D_MODEL), 1.0),
        'c_ctx': normal(ks[3], (D_MODEL,), 1.0),
        'ada_w': normal(ks[4], (DEPTH, D_MODEL, 6 * D_MODEL), 0.5 * D_MODEL ** -0.5),
        'ada_b': normal(ks[5], (DEPTH, 6 * D_MODEL), 0.01),
        'norm_mix_g': gain(ks[6], (DEPTH, D_MODEL)),
        'norm_ffn_g': gain(ks[7], (DEPTH, D_MODEL)),
        'ffn_w1': normal(ks[8], (DEPTH, D_MODEL, D_FF_2), D_MODEL ** -0.5),
        'ffn_w2': normal(ks[9], (DEPTH, D_FF_2, D_MODEL), D_FF_2 ** -0.5),
        'dn_w_in': normal(ks[10], (n_a, D_MODEL, DN_IN_DIM), D_MODEL ** -0.5),
        'dn_conv_w': normal(ks[11], (n_a, DN_QKV_DIM, SHORT_CONV), SHORT_CONV ** -0.5),
        'dn_a_log': jnp.log(jax.random.uniform(ks[13], (n_a, 2, DN_V_HEADS), F32, 1.0, 16.0)),
        'dn_dt_bias': dt + jnp.log(-jnp.expm1(-dt)),
        'dn_norm_g': gain(ks[14], (n_a, DN_HEAD_V)),
        'dn_w_out': normal(ks[15], (n_a, DN_V_DIM, D_MODEL), DN_V_DIM ** -0.5),
        'gla_w_in': normal(ks[16], (n_b, D_MODEL, GLA_IN_DIM), D_MODEL ** -0.5),
        'gla_gate_w2': normal(ks[17], (n_b, 2, GLA_GATE_RANK, GLA_K_DIM), GLA_GATE_RANK ** -0.5),
        'gla_gate_b2': normal(ks[18], (n_b, 2, GLA_K_DIM), 0.1),
        'gla_norm_g': gain(ks[19], (n_b, GLA_HEAD_V)),
        'gla_w_out': normal(ks[20], (n_b, GLA_V_DIM, D_MODEL), GLA_V_DIM ** -0.5),
        'attn_w_in': normal(ks[21], (n_c, D_MODEL, ATTN_IN_DIM), D_MODEL ** -0.5),
        'attn_q_norm_g': gain(ks[22], (n_c, ATTN_HEAD_DIM)),
        'attn_k_norm_g': gain(ks[23], (n_c, ATTN_HEAD_DIM)),
        'attn_w_out': normal(ks[24], (n_c, ATTN_Q_DIM, D_MODEL), ATTN_Q_DIM ** -0.5),
    }

def second_block(x, c, ctx, c_ctx, ada_w, ada_b, norm_mix_g, norm_ffn_g, ffn_w1, ffn_w2,
              dn_w_in, dn_conv_w, dn_a_log, dn_dt_bias, dn_norm_g, dn_w_out,
              gla_w_in, gla_gate_w2, gla_gate_b2, gla_norm_g, gla_w_out,
              attn_w_in, attn_q_norm_g, attn_k_norm_g, attn_w_out):
    n_tok = x.shape[1]
    ROWS = n_tok // GRID_W
    rope = axial_rope_tables(ROWS)
    for i in range(DEPTH):
        with_ctx_out = i < DEPTH - 1
        mix, slot = i % N_MIXERS, i // N_MIXERS
        mod_x = jnp.split((jax.nn.silu(c) @ ada_w[i] + ada_b[i])[:, None, :], 6, axis=-1)
        mod_c = jnp.split(jax.nn.silu(c_ctx) @ ada_w[i] + ada_b[i], 6, axis=-1)
        hx = modulate_2(rms_norm_2(x, norm_mix_g[i]), mod_x[0], mod_x[1])
        hc = modulate_2(rms_norm_2(ctx, norm_mix_g[i]), mod_c[0], mod_c[1])
        if mix == 0:
            yx, yc = deltanet_mixer(hx, hc, dn_w_in[slot], dn_conv_w[slot], dn_a_log[slot], dn_dt_bias[slot],
                                    dn_norm_g[slot], dn_w_out[slot], with_ctx_out)
        elif mix == 1:
            yx, yc = gla_mixer(hx, hc, gla_w_in[slot], gla_gate_w2[slot], gla_gate_b2[slot],
                               gla_norm_g[slot], gla_w_out[slot], with_ctx_out)
        else:
            yx, yc = attention_mixer(hx, hc, attn_w_in[slot], attn_q_norm_g[slot], attn_k_norm_g[slot],
                                     attn_w_out[slot], rope, with_ctx_out)
        x = x + mod_x[2] * yx
        hx = modulate_2(rms_norm_2(x, norm_ffn_g[i]), mod_x[3], mod_x[4])
        x = x + mod_x[5] * squared_relu_ffn(hx, ffn_w1[i], ffn_w2[i])
        if with_ctx_out:
            ctx = ctx + mod_c[2] * yc
            hc = modulate_2(rms_norm_2(ctx, norm_ffn_g[i]), mod_c[3], mod_c[4])
            ctx = ctx + mod_c[5] * squared_relu_ffn(hc, ffn_w1[i], ffn_w2[i])
    return x


def setup_inputs(seed=0):
    out = dict(first_inputs(seed))
    for name, value in second_inputs(seed + 1).items():
        if name != "x":
            out[name + "_2"] = value
    return out


def reference(
    x, c, ctx, c_ctx, norm1_g, norm2_g, w_mod, b_mod, w_in, q_norm_g, kv_norm_g, w_uq, w_ukv,
    hy_conv_w, hy_conv_b, hy_w1, hy_b1, hy_freq, hy_w2, hy_b2, hy_w3, hy_d, w_out, w_mlp1,
    w_mlp2, final_norm_g, c_2, ctx_2, c_ctx_2, ada_w_2, ada_b_2, norm_mix_g_2, norm_ffn_g_2,
    ffn_w1_2, ffn_w2_2, dn_w_in_2, dn_conv_w_2, dn_a_log_2, dn_dt_bias_2, dn_norm_g_2,
    dn_w_out_2, gla_w_in_2, gla_gate_w2_2, gla_gate_b2_2, gla_norm_g_2, gla_w_out_2,
    attn_w_in_2, attn_q_norm_g_2, attn_k_norm_g_2, attn_w_out_2,
):
    x = first_block(
        x, c, ctx, c_ctx, norm1_g, norm2_g, w_mod, b_mod, w_in, q_norm_g, kv_norm_g, w_uq,
        w_ukv, hy_conv_w, hy_conv_b, hy_w1, hy_b1, hy_freq, hy_w2, hy_b2, hy_w3, hy_d, w_out,
        w_mlp1, w_mlp2, final_norm_g,
    )
    return second_block(
        x, c_2, ctx_2, c_ctx_2, ada_w_2, ada_b_2, norm_mix_g_2, norm_ffn_g_2, ffn_w1_2,
        ffn_w2_2, dn_w_in_2, dn_conv_w_2, dn_a_log_2, dn_dt_bias_2, dn_norm_g_2, dn_w_out_2,
        gla_w_in_2, gla_gate_w2_2, gla_gate_b2_2, gla_norm_g_2, gla_w_out_2, attn_w_in_2,
        attn_q_norm_g_2, attn_k_norm_g_2, attn_w_out_2,
    )


_drawn_inputs = setup_inputs


def setup_inputs(seed=0):
    import zlib

    import numpy as np

    out = dict(_drawn_inputs(seed))
    spreads = {}
    factors = {'ctx': 3.406,
     'norm1_g': 3.678,
     'q_norm_g': 8.0,
     'kv_norm_g': 8.0,
     'hy_conv_b': 8.0,
     'hy_b1': 8.0,
     'hy_freq': 8.0,
     'hy_b2': 8.0,
     'norm_mix_g_2': 5.967,
     'norm_ffn_g_2': 4.451,
     'dn_norm_g_2': 8.0,
     'gla_gate_b2_2': 5.646,
     'gla_norm_g_2': 8.0}
    for name, (base, spread) in spreads.items():
        noise = np.random.default_rng([zlib.crc32(name.encode()), seed]).standard_normal(out[name].shape)
        drawn = base * np.exp(spread * noise) if base else spread * noise
        out[name] = jnp.asarray(drawn.astype(out[name].dtype))
    for name, factor in factors.items():
        out[name] = (out[name] * factor).astype(out[name].dtype)
    return out
```

```python
from contextlib import ExitStack, contextmanager

import numpy as np

import concourse.bass as bass
from concourse import mybir

F32 = mybir.dt.float32
F32R = mybir.dt.float32r
I32 = mybir.dt.int32
ALU = mybir.AluOpType
ACT = mybir.ActivationFunctionType
AX = mybir.AxisListType

P = 128
D = 1024
KD = D // P
L = 256
T2 = 2 * L
NT = T2 // P
DEPTH = 2
EPS = 1e-6
NMOD = 6
MT = NMOD * KD
HEADS, NOPE, ROPE, VH = 8, 64, 32, 64
QLORA, KVLORA = 384, 256
FW = 256
OFF_KV, OFF_KR, OFF_F, OFF_H = 384, 640, 672, 928
FILT_EMB, FILT = 33, 64
HT = 4 * D // P
SLAB = 2048
RING = 4

PQ, PKR, PKV, PF, PH, NPX = 0, 3, 4, 6, 8, 14

DNH, DNK = 16, 8
GH, GV = 4, 256
LEV = 7


def first_constants():
    c = {}
    f = np.float64
    t = np.arange(L)
    inv = np.float32(10000.0) ** (-np.arange(0, 16, 2, dtype=np.float32) / np.float32(16))
    row, col = (t // 64).astype(np.float32), (t % 64).astype(np.float32)
    ang = np.concatenate([row[:, None] * inv, col[:, None] * inv], 1)
    cos, sin = np.cos(ang.astype(f)), np.sin(ang.astype(f))
    rope_cs = np.zeros((P, L))
    for r in range(32):
        axis, j = r // 16, r % 16
        a = axis * 8 + j % 8
        rope_cs[64 + r] = cos[:, a]
        rope_cs[96 + r] = sin[:, a] * (-1 if j < 8 else 1)
    c["rope"] = rope_cs
    k = np.arange(64)
    a64 = 2 * np.pi * np.outer(k, k) / 64
    cs, sn = np.cos(a64) / 128, np.sin(a64) / 128
    z = np.zeros((64, 64))
    c["dft_feat"] = np.concatenate([np.block([[cs, z], [z, cs]]), np.block([[sn, z], [z, sn]])], 1)
    aL = 2 * np.pi * (np.outer(t, t) % L) / L
    tiles = lambda m: m.reshape(2, P, -1).transpose(1, 0, 2).reshape(P, -1)
    c["dft_cos"] = tiles(np.cos(aL))
    c["dft_nsin"] = tiles(-np.sin(aL))
    w = np.arange(L)
    odd = np.pi * ((np.outer(t, 2 * w + 1)) % (2 * T2)) / T2
    c["odd_cos"] = tiles(np.cos(odd))
    c["odd_nsin"] = tiles(-np.sin(odd))
    c["inv_cos"] = tiles(np.cos(odd).T / L)
    c["inv_nsin"] = tiles(-np.sin(odd).T / L)
    tt = np.linspace(0.0, 1.0, L, dtype=np.float32)[:, None]
    fr = np.linspace(1e-4, 15, 16, dtype=np.float32)
    ang = (np.float32(2.0 * np.pi) * np.arange(L, dtype=np.float32)[:, None] / np.float32(L) * fr).astype(f)
    emb = np.concatenate([tt, np.cos(ang), -np.sin(ang)], 1)
    c["filter_emb"] = np.concatenate([emb.T, np.zeros((P - FILT_EMB, L))], 0)
    d0, d1 = np.log(1e-2) / 1.5, np.log(1e-2) / 0.3
    deltas = np.abs(np.linspace(d0, d1, FW, dtype=np.float32)).astype(f)
    decay = np.exp(-tt.astype(f) * deltas)
    both = np.concatenate([decay, decay], 1)
    both[0, FW:] = 0
    c["decay"] = tiles(both)
    return {n: np.ascontiguousarray(a, np.float32) for n, a in c.items()}


def second_constants():
    c = {}
    i = np.arange(P)
    a, b = i[:, None], i[None, :]
    c["incl"] = np.concatenate([a <= b, a >= b], 1)
    c["after"] = np.concatenate([a > b, a < b], 1)
    lower = [(a >> n) % 2 * ((b >> n) % 2 == 0) * ((a >> (n + 1)) == (b >> (n + 1))) for n in range(LEV)]
    c["lower"] = np.concatenate([a == b] + lower, 1)
    c["upper"] = np.concatenate([a == b] + [m.T for m in lower], 1)
    fwd, bwd = [a <= b], [a >= b]
    for n in range(LEV):
        odd = (b >> n) % 2 == 1
        start = np.where(odd, b >> n << n, (b >> n) + 1 << n)
        end = start + (1 << n)
        fwd.append(np.where(odd, (a >= start) & (a <= b), (a > b) & (a < start)))
        bwd.append(np.where(odd, (a >= start) & (a < b), (a >= b) & (a < start)))
    c["exps"] = np.concatenate(fwd + bwd, 1)
    return {n: np.ascontiguousarray(m, np.float32) for n, m in c.items()}


def columns(table):
    at, out = 0, {}
    for n, w in table:
        out[n] = (at, w)
        at += w
    return out, at


FIRST = [("rope", 256), ("dft_feat", 256), ("dft_cos", 512), ("dft_nsin", 512), ("odd_cos", 512), ("odd_nsin", 512),
         ("inv_cos", 512), ("inv_nsin", 512), ("filter_emb", 256), ("decay", 1024)]
SECOND = [("incl", 256), ("after", 256), ("lower", 1024), ("upper", 1024), ("exps", 2048)]
VECS = [("c1", 16), ("c2", 16), ("g1", 32), ("g2", 32), ("b_mod", 2 * 2 * MT), ("qg", 6), ("kvg", 4), ("cw", 2 * 18),
        ("cb", 12), ("hyd", 4), ("gf", 8), ("b_ada", 2 * 2 * MT), ("gm", 32), ("gn", 32), ("hb1", 2), ("hfreq", 2),
        ("hb2", 2), ("dncw", 160), ("dng", 1), ("glag", 2), ("dt", 32), ("alog", 32)]
VCOL, NVEC = columns(VECS)
CCOL, NCST = columns(FIRST)
CCOL2, NCST2 = columns(SECOND)
CCOL.update(CCOL2)
MOD_SLABS, IN_SLABS, UP_SLABS, OUT_SLABS, MLP_SLABS = 24, 7, 3, 4, 16


class View:

    def __init__(self, own):
        self.own = own
        self.base, self.within, self.stages = {}, {}, 0
        self.it, self.per = 0, {}

    def __getitem__(self, name):
        return self.base.get(name, 0) + (self.it * self.per[name] if name in self.per else 0)

    def filled(self, b, nth=0):
        return self[b] + nth + 1

    def free(self, b, nth=0):
        return self[b] + nth + 1

    def freed(self, b, nth=1):
        return self[b] + nth + 1

    def of(self, name, nth=1):
        return self[name] + nth

    def step(self):
        own = self.own + "_step"
        self.within[own] = self.within.get(own, 0) + 1
        return 1

    def steps(self):
        own = self.own + "_step"
        return self[own] + self.within.get(own, 0)

    @contextmanager
    def loop(self, it, iterations, per):
        self.it, self.per = it, per
        yield
        own = self.own + "_step"
        assert self.within.get(own, 0) == per.get(own, 0), (own, self.within.get(own, 0))
        for n, k in per.items():
            self.base[n] = self.base.get(n, 0) + k * iterations
        self.it, self.per, self.within = 0, {}, {}

    def pass_over(self, uses, stages=1):
        for n, k in uses.items():
            self.base[n] = self.base.get(n, 0) + k
        self.stages += stages

    def place(self, j, *loop):
        return (self.base.get("slab", 0) + j) % RING

    def landed(self, j, i=0, per=0):
        return i * (16 * per // RING) + 16 * ((self.base.get("slab", 0) + j) // RING + 1)

    def end(self, uses):
        own = self.own + "_step"
        self.base[own] = self[own] + self.within.get(own, 0)
        for n, k in uses.items():
            self.base[n] = self.base.get(n, 0) + k
        self.within = {}
        self.stages += 1


def banks(tiles, n=8, first=0):
    out = {}
    for t in range(tiles):
        b = first + t % n
        out[b] = out.get(b, 0) + 1
    return out


def build(nc, A, out):
    with ExitStack() as ctx:
        def sb(name, shape, dt=F32):
            return ctx.enter_context(nc.sbuf_tensor(name, shape, dt))

        X = sb("X", [P, KD, T2])
        H = sb("H", [P, KD, T2])
        ring = sb("ring", [P, RING, SLAB])
        C = sb("C", [P, NCST])
        V = sb("V", [P, NVEC])
        M = sb("M", [P, MT * 2])
        SA = sb("SA", [P, 2, KD * 2])
        cs = sb("cs", [P, 2, KD * 2])
        ones = sb("ones", [P, P])
        ident = sb("ident", [P, P])
        RS = sb("RS", [P, 2, T2])
        with ExitStack() as beneath:
            parts = {n: beneath.enter_context(nc.sbuf_tensor(n, shape, F32R)) for n, shape in (
                ("h_high", [P, KD, T2]), ("h_low", [P, KD, T2]), ("hidden_high", [P, KD, T2]),
                ("hidden_low", [P, KD, T2]), ("w_high", [P, 2, SLAB]), ("w_low", [P, 2, SLAB]))}
        H_HIGH, H_LOW, HID_HIGH, HID_LOW, W_HIGH, W_LOW = parts.values()
        arena = sb("arena", [P, 29600])
        ps = ctx.enter_context(nc.psum_tensor("ps", [P, 8, 512], F32))

        def part(at, *shape):
            n = int(np.prod(shape))
            v = arena[:, at:at + n]
            if len(shape) == 2:
                v = v.rearrange("p (a b) -> p a b", b=shape[1])
            if len(shape) == 3:
                v = v.rearrange("p (a b c) -> p a b c", b=shape[1], c=shape[2])
            return v

        ROWS = part(0, 8, 256)

        PX = part(0, NPX, T2)
        QT = part(7168, HEADS, T2)
        KT = part(11264, HEADS, T2)
        VT = part(15360, NT, HEADS * VH)
        MIX = part(17408, KD, T2)
        PR = part(21504, 2, T2)
        PT = part(22528, 2, T2)
        RT = part(23552, HEADS, L)
        HYW = part(25600, DEPTH, 640)
        ST = part(26880, 4, 32)
        YF = part(7168, NT, 512)
        U = part(9216, 6, T2)
        Z = part(12288, 2, T2)
        ZT = part(13312, 2, 512)
        HF = part(14336, 2, 512)
        HS = part(15360, 2, 512)
        KS = part(16384, 2, 512)
        ZS = part(21504, 4, 512)
        YS = part(23552, 4, 512)
        SN = part(27008, 6, 256)
        KA = part(28544, 2, 256)
        RK = part(29056, 8)
        RELU = part(24576, 2, T2)
        SQR = part(27008, 2, T2)

        QK = part(0, 16, T2)
        VV = part(8192, DNH, T2)
        OO = part(16384, DNH, T2)
        QKV = part(0, 32, T2)
        SS = part(24576, DNH, P)
        KTOK = part(26624, 2, 256)
        SC = part(27136, 8, P)
        TG = part(28160, 3, P)
        MS = part(28544, 64)
        CB = part(16384, 4, 520)
        CO = part(18464, 4, T2)
        SQ = part(20512, 2, T2)
        RR = part(21536, 4, T2)
        SG_, SB_, SNB, SNEG, SEG, SBT, SET = range(7)
        UB = [X, H]
        GT, DT, PTT, TM, TT, ZM, AM, KQ = range(8)

        GK = part(0, NT, 1024)
        KTK = part(4096, NT, 512)
        VTK = part(6144, NT, 1024)
        QF = part(10240, GH, L)
        KF = part(11264, GH, L)
        SG = part(12288, GH, GV)
        EX = part(13312, 2, 1024)
        QX = part(15360, 2, 1024)
        KX = part(17408, 2, 1024)
        AP_ = part(19456, 2, 1024)
        ATG = part(21504, 2, P)
        KTL = part(21760, 2, 512)
        ETG = part(22784, 2, GH)
        LOW = part(22792, T2)
        GW = part(23304, 1536)
        GMIX = part(24840, KD, L)
        GT1 = part(26888, 512)
        GT2 = part(27400, 512)
        GMS = part(27912, 8)
        GSQ = part(27920, 1024)
        OG = H[:, 0:4, :].rearrange("p a b -> p (a b)").rearrange("p (t f) -> p t f", t=2)
        GZ = H[:, 4:8, :].rearrange("p a b -> p (a b)").rearrange("p (f t) -> p f t", t=L)

        names = [f"filled{b}" for b in range(8)] + [f"freed{b}" for b in range(8)] + [f"landed{s}" for s in range(RING)]
        names += ["slab_begun", "loaded", "squares", "root", "scaled", "maxed", "normed", "stored", "prepared",
                  "sines", "reduced", "first_loaded", "zmul", "prod", "affine", "decayed", "convolved", "silu",
                  "gates", "gt0", "gt1", "kq0", "kq1", "pt0", "pt1", "eye0", "eye1", "ti0", "ti1", "spilled", "restored",
                  "second_loaded", "rows_zeroed", "abs", "ktl", "qx", "at", "sq", "scales",
                  "h_high", "h_split", "w_high", "w_split", "squared", "hidden_high", "hidden_split"]
        for e in ("pe", "act", "dve", "pool"):
            names += [e + "_step", e + "_stage_end"]
        sems = {n: ctx.enter_context(nc.semaphore(n)) for n in names}
        filled = [sems[f"filled{b}"] for b in range(8)]
        freed = [sems[f"freed{b}"] for b in range(8)]
        landed = [sems[f"landed{s}"] for s in range(RING)]
        pe_stage_end, act_stage_end, dve_stage_end = (sems[e + "_stage_end"] for e in ("pe", "act", "dve"))
        act_step, dve_step, pool_step = (sems[e + "_step"] for e in ("act", "dve", "pool"))
        block = ctx.enter_context(nc.Block())

        def vec(name, i=0, n=1):
            at = VCOL[name][0] + i
            return V[:, at:at + n]

        def cst(name, a, b):
            at = CCOL[name][0]
            return C[:, at + a:at + b]

        def slab_view(s, kt, nc_, off=0):
            return ring[:, s, off:off + kt * nc_].rearrange("p (k n) -> p k n", k=kt)

        U_MOD = {**{b: 6 for b in range(8)}, "slab": MOD_SLABS, "rows_zeroed": 1}
        U_NORM = {0: 1, "squares": KD, "root": 1, "scaled": KD}
        U_IN = {**banks(14), "slab": IN_SLABS}
        U_LORA = {0: 1, 1: 1, "squares": 5, "root": 2}
        U_UP = {**banks(20), "slab": UP_SLABS}
        U_OUT = {**banks(8), "slab": OUT_SLABS}
        U_MLP = {**{b: 8 for b in range(8)}, "slab": 2 * MLP_SLABS, "h_high": KD, "h_split": KD,
                 "w_high": 2 * MLP_SLABS, "w_split": 2 * MLP_SLABS, "squared": HT, "hidden_high": HT, "hidden_split": HT}
        U_FNORM = {0: 1, "squares": KD, "root": 1}

        def attn_units(l):
            return [(s, h, q) for s in range(2 if l == 0 else 1) for h in range(HEADS) for q in range(2)]

        def u_attn(l):
            n = len(attn_units(l))
            return {0: n // 2, 1: n // 2, 2: n // 2, 3: n // 2, 4: n // 2, 5: n // 2,
                    "maxed": n, "normed": n}

        def u_fnet(l):
            return banks(8 if l == 0 else 4)

        def u_filter(l):
            return {0: 1, 1: 1, 2: 1, 3: 1, 4: 1, "reduced": 2, "sines": 2, "decayed": 1}

        def u_hyena(l):
            both = 2 if seqs(l) == 2 else 1
            return {0: 2, 1: 2, 2: both, 3: both, 4: 1, 5: 1, 6: 1, 7: 1, "affine": 6, "zmul": 1, "prod": 1}

        def seqs(l):
            return 2 if l == 0 else 1

        def pe_slab_gemm(pe, v, j, s, tiles, kt, rhs, T, b0):
            w = slab_view(s, kt, tiles["cols"])
            for n, (c0, m, tok) in enumerate(tiles["list"]):
                b = (b0 + n) % 8
                pe.wait_ge(freed[b], v.free(b, (b0 + n) // 8))
                for k in range(kt):
                    ins = nc.tensor.matmul(ps[0:m, b, 0:tok], w[:, k, c0:c0 + m], rhs(k)[:, 0:tok],
                                           start=(k == 0), stop=(k == kt - 1))
                    if n == 0 and k == 0:
                        ins.then_inc(sems["slab_begun"], 1)
                ins.then_inc(filled[b], 1)

        def pe_mod(pe, v, blk):
            with pe.Fori(0, 3) as i:
                for u in range(9):
                    if u < 8:
                        s = v.place(u, i, 8)
                        w = slab_view(s, KD, 256)
                        pe.wait_ge(landed[s], v.landed(u, i, 8))
                        pe.wait_ge(freed[u % 4], i * 2 + v.free(u % 4, u // 4))
                        for k in range(KD):
                            ins = nc.tensor.matmul(ps[0:2, u % 4, 0:256], cs[:, blk, 2 * k:2 * k + 2], w[:, k, :],
                                                   start=(k == 0), stop=(k == KD - 1))
                            if k == 0:
                                ins.then_inc(sems["slab_begun"], 1)
                        ins.then_inc(filled[u % 4], 1)
                    if u > 0:
                        r, b = u - 1, 4 + (u - 1) % 4
                        pe.wait_ge(freed[r % 4], i * 2 + v.freed(r % 4, r // 4 + 1))
                        pe.wait_ge(freed[b], i * 2 + v.free(b, r // 4))
                        for t in range(2):
                            ins = nc.tensor.transpose(ps[:, b, t * P:(t + 1) * P], ROWS[:, r, t * P:(t + 1) * P], ident[:])
                        ins.then_inc(filled[b], 1)
            v.end(U_MOD)
            pe.drain().then_inc(pe_stage_end, 1)
            pe.wait_ge(act_stage_end, v.stages)
            pe.wait_ge(dve_stage_end, v.stages)

        def pe_norm(pe, v, T):
            pe.wait_ge(freed[0], v.free(0))
            for k in range(KD):
                pe.wait_ge(sems["squares"], v.of("squares", k + 1))
                ins = nc.tensor.matmul(ps[:, 0, 0:T], ones[:], H[:, k, 0:T], start=(k == 0), stop=(k == KD - 1))
            ins.then_inc(filled[0], 1)
            v.end(U_NORM)
            pe.drain().then_inc(pe_stage_end, 1)
            pe.wait_ge(act_stage_end, v.stages)
            pe.wait_ge(dve_stage_end, v.stages)

        def pe_in(pe, v, l):
            T = T2 if l == 0 else L
            b = 0
            for j in range(IN_SLABS):
                s = v.place(j)
                pe.wait_ge(landed[s], v.landed(j))
                toks = [(0, P, T), (P, P, T)]
                if j == 1:
                    toks = [(0, P, T), (P, P, T2)]
                if j == 2:
                    toks = [(0, P, T2), (P, P, T2)]
                pe_slab_gemm(pe, v, j, s, {"cols": 256, "list": toks}, KD, lambda k: H[:, k, :], T, b)
                b += 2
            v.end(U_IN)
            pe.drain().then_inc(pe_stage_end, 1)
            pe.wait_ge(act_stage_end, v.stages)
            pe.wait_ge(dve_stage_end, v.stages)

        def pe_lora(pe, v, l):
            T = T2 if l == 0 else L
            for b, (k0, n, tok) in enumerate(((0, 3, T), (3, 2, T2))):
                pe.wait_ge(freed[b], v.free(b))
                for k in range(n):
                    pe.wait_ge(sems["squares"], v.of("squares", k0 + k + 1))
                    ins = nc.tensor.matmul(ps[:, b, 0:tok], ones[:], H[:, k0 + k, 0:tok], start=(k == 0), stop=(k == n - 1))
                ins.then_inc(filled[b], 1)
            v.end(U_LORA)
            pe.drain().then_inc(pe_stage_end, 1)
            pe.wait_ge(act_stage_end, v.stages)
            pe.wait_ge(dve_stage_end, v.stages)

        def pe_up(pe, v, l):
            T = T2 if l == 0 else L
            for j in range(2):
                s = v.place(j)
                pe.wait_ge(landed[s], v.landed(j))
                pe_slab_gemm(pe, v, j, s, {"cols": 512, "list": [(P * a, P, T) for a in range(4)]}, 3,
                             lambda k: PX[:, PQ + k, :], T, 4 * j)
            s = v.place(2)
            pe.wait_ge(landed[s], v.landed(2))
            wk, wv = slab_view(s, 2, 512), slab_view(s, 2, 512, 1024)
            for h in range(HEADS):
                pe.wait_ge(freed[h], v.free(h, 1))
                for k in range(2):
                    ins = nc.tensor.matmul(ps[0:NOPE, h, :], wk[:, k, h * NOPE:(h + 1) * NOPE], PX[:, PKV + k, :],
                                           start=(k == 0), stop=(k == 1))
                    if h == 0 and k == 0:
                        ins.then_inc(sems["slab_begun"], 1)
                ins.then_inc(filled[h], 1)
            for t in range(NT):
                pe.wait_ge(freed[t], v.free(t, 2))
                for k in range(2):
                    ins = nc.tensor.matmul(ps[:, t, :], PX[:, PKV + k, t * P:(t + 1) * P], wv[:, k, :],
                                           start=(k == 0), stop=(k == 1))
                ins.then_inc(filled[t], 1)
            v.end(U_UP)
            pe.drain().then_inc(pe_stage_end, 1)
            pe.wait_ge(act_stage_end, v.stages)
            pe.wait_ge(dve_stage_end, v.stages)

        def keys_of(s):
            return (0, T2) if s == 0 else (L, L)

        def pe_attn(pe, v, l):
            units = attn_units(l)
            n = len(units)
            for i in range(n + 2):
                if i < n:
                    s, h, q = units[i]
                    k0, kn = keys_of(s)
                    b = i % 2
                    pe.wait_ge(freed[b], v.free(b, i // 2))
                    q0 = s * L + q * P
                    ins = nc.tensor.matmul(ps[:, b, 0:kn], QT[0:96, h, q0:q0 + P], KT[0:96, h, k0:k0 + kn],
                                           start=True, stop=True)
                    ins.then_inc(filled[b], 1)
                if 1 <= i <= n:
                    u = i - 1
                    s, h, q = units[u]
                    kn = keys_of(s)[1]
                    b = 2 + u % 2
                    pe.wait_ge(freed[b], v.free(b, u // 2))
                    pe.wait_ge(sems["normed"], v.of("normed", u + 1))
                    for a in range(kn // P):
                        ins = nc.tensor.transpose(ps[:, b, a * P:(a + 1) * P], PR[:, u % 2, a * P:(a + 1) * P], ident[:])
                    ins.then_inc(filled[b], 1)
                if i >= 2:
                    u = i - 2
                    s, h, q = units[u]
                    k0, kn = keys_of(s)
                    b = 4 + u % 2
                    pe.wait_ge(freed[b], v.free(b, u // 2))
                    pe.wait_ge(freed[2 + u % 2], v.freed(2 + u % 2, u // 2 + 1))
                    for a in range(kn // P):
                        hp = (h // 2) * P
                        ins = nc.tensor.matmul(ps[:, b, 0:P], VT[:, k0 // P + a, hp:hp + P], PT[:, u % 2, a * P:(a + 1) * P],
                                               start=(a == 0), stop=(a == kn // P - 1))
                    ins.then_inc(filled[b], 1)
            v.end(u_attn(l))
            pe.drain().then_inc(pe_stage_end, 1)
            pe.wait_ge(act_stage_end, v.stages)
            pe.wait_ge(dve_stage_end, v.stages)

        def pe_fnet(pe, v, l):
            n1 = 2 * seqs(l)
            for t in range(n1):
                pe.wait_ge(freed[t], v.free(t))
                for f in range(2):
                    ins = nc.tensor.matmul(ps[:, t, f * 256:(f + 1) * 256], PX[:, PF + f, t * P:(t + 1) * P],
                                           cst("dft_feat", 0, 256), start=True, stop=True)
                ins.then_inc(filled[t], 1)
            for u in range(n1):
                s, f = u // 2, u % 2
                b = (n1 + u) % 8
                pe.wait_ge(freed[b], v.free(b))
                for a in range(2):
                    pe.wait_ge(freed[2 * s + a], v.free(2 * s + a, 1))
                    nc.tensor.matmul(ps[:, b, 0:256], YF[:, 2 * s + a, f * 256:f * 256 + P],
                                     cst("dft_cos", a * 256, a * 256 + 256), start=(a == 0), stop=False)
                    ins = nc.tensor.matmul(ps[:, b, 0:256], YF[:, 2 * s + a, f * 256 + P:f * 256 + 2 * P],
                                           cst("dft_nsin", a * 256, a * 256 + 256), start=False, stop=(a == 1))
                ins.then_inc(filled[b], 1)
            v.end(u_fnet(l))
            pe.drain().then_inc(pe_stage_end, 1)
            pe.wait_ge(act_stage_end, v.stages)
            pe.wait_ge(dve_stage_end, v.stages)

        def pe_filter(pe, v, l):
            pe.wait_ge(freed[0], v.free(0))
            nc.tensor.matmul(ps[0:FILT, 0, 0:L], HYW[0:FILT_EMB, l, 0:64], C[0:FILT_EMB, CCOL["filter_emb"][0]:CCOL["filter_emb"][0] + L],
                                     start=True, stop=True).then_inc(filled[0], 1)
            pe.wait_ge(sems["sines"], v.of("sines", 1))
            pe.wait_ge(freed[1], v.free(1))
            nc.tensor.matmul(ps[0:FILT, 1, 0:L], HYW[0:FILT, l, 64:128], SN[0:FILT, 4, :], start=True, stop=True).then_inc(filled[1], 1)
            pe.wait_ge(sems["sines"], v.of("sines", 2))
            for a in range(2):
                pe.wait_ge(freed[2 + a], v.free(2 + a))
                nc.tensor.matmul(ps[:, 2 + a, :], SN[0:FILT, 5, a * P:(a + 1) * P], HYW[0:FILT, l, 128:640],
                                         start=True, stop=True).then_inc(filled[2 + a], 1)
            pe.wait_ge(sems["decayed"], v.of("decayed", 1))
            pe.wait_ge(freed[4], v.free(4))
            for c in range(2):
                for a in range(2):
                    ins = nc.tensor.matmul(ps[:, 4, c:c + 1], KA[:, a, c * P:(c + 1) * P], ones[:, 0:1], start=(a == 0), stop=(a == 1))
            ins.then_inc(filled[4], 1)
            v.end(u_filter(l))
            pe.drain().then_inc(pe_stage_end, 1)
            pe.wait_ge(act_stage_end, v.stages)
            pe.wait_ge(dve_stage_end, v.stages)

        def pe_hyena(pe, v, l):
            S = seqs(l)
            for f in range(2):
                pe.wait_ge(freed[4 + f], v.free(4 + f))
                for r in range(2):
                    for a in range(2):
                        tab = "odd_cos" if r == 0 else "odd_nsin"
                        ins = nc.tensor.matmul(ps[:, 4 + f, r * 256:(r + 1) * 256], cst(tab, a * 256 + f * P, a * 256 + (f + 1) * P),
                                               HS[:, a, r * 256:(r + 1) * 256], start=(a == 0), stop=(a == 1))
                ins.then_inc(filled[4 + f], 1)
            pe.wait_ge(sems["zmul"], v.of("zmul", 1))
            for a in range(2):
                pe.wait_ge(freed[6 + a], v.free(6 + a))
                for s in range(S):
                    for c in range(2):
                        ins = nc.tensor.transpose(ps[:, 6 + a, s * 256 + c * P:s * 256 + (c + 1) * P],
                                                  Z[:, c, s * L + a * P:s * L + (a + 1) * P], ident[:])
                ins.then_inc(filled[6 + a], 1)
            pe.wait_ge(freed[6], v.freed(6))
            pe.wait_ge(freed[7], v.freed(7))
            for f in range(2):
                for r in range(2):
                    b = 2 * f + r
                    pe.wait_ge(freed[b], v.free(b))
                    tab = "odd_cos" if r == 0 else "odd_nsin"
                    for a in range(2):
                        ins = nc.tensor.matmul(ps[:, b, 0:S * 256], cst(tab, a * 256 + f * P, a * 256 + (f + 1) * P),
                                               ZT[:, a, 0:S * 256], start=(a == 0), stop=(a == 1))
                    ins.then_inc(filled[b], 1)
            pe.wait_ge(sems["prod"], v.of("prod", 1))
            for u in range(4):
                c, s = u % 2, u // 2
                if s >= S:
                    continue
                b = (0, 1, 2, 3)[u]
                pe.wait_ge(freed[b], v.free(b, 1))
                for f in range(2):
                    for r in range(2):
                        tab = "inv_cos" if r == 0 else "inv_nsin"
                        ins = nc.tensor.matmul(ps[:, b, 0:256], YS[:, 2 * f + r, s * 256 + c * P:s * 256 + (c + 1) * P],
                                               cst(tab, f * 256, f * 256 + 256), start=(f == 0 and r == 0), stop=(f == 1 and r == 1))
                ins.then_inc(filled[b], 1)
            v.end(u_hyena(l))
            pe.drain().then_inc(pe_stage_end, 1)
            pe.wait_ge(act_stage_end, v.stages)
            pe.wait_ge(dve_stage_end, v.stages)

        def pe_out(pe, v, T, mix):
            for j in range(OUT_SLABS):
                s = v.place(j)
                pe.wait_ge(landed[s], v.landed(j))
                pe_slab_gemm(pe, v, j, s, {"cols": 256, "list": [(0, P, T), (P, P, T)]}, KD, lambda k: mix[:, k, :], T, 2 * j)
            v.end(U_OUT)
            pe.drain().then_inc(pe_stage_end, 1)
            pe.wait_ge(act_stage_end, v.stages)
            pe.wait_ge(dve_stage_end, v.stages)

        def pe_mlp(pe, v, T):
            with pe.Fori(0, 4) as i:
                for j in range(8):
                    pe.wait_ge(sems["w_split"], i * 8 + v.of("w_split", j + 1))
                    for t in range(2):
                        b = 2 * (j % 4) + t
                        pe.wait_ge(freed[b], i * 2 + v.free(b, j // 4))
                        for k in range(KD):
                            if j == 0 and t == 0:
                                pe.wait_ge(sems["h_split"], v.of("h_split", k + 1))
                            if j == 4 and t == 0:
                                pe.wait_ge(sems["hidden_split"], i * 8 + v.of("hidden_split", k + 1))
                            ws = slice(k * 256 + t * P, k * 256 + (t + 1) * P)
                            high, low = (H_HIGH, H_LOW) if j < 4 else (HID_HIGH, HID_LOW)
                            ins = nc.tensor.matmul(ps[:, b, 0:T], W_HIGH[:, j % 2, ws], high[:, k, 0:T], start=(k == 0), stop=False)
                            if t == 0 and k == 0:
                                ins.then_inc(sems["slab_begun"], 1)
                            nc.tensor.matmul(ps[:, b, 0:T], W_HIGH[:, j % 2, ws], low[:, k, 0:T], start=False, stop=False)
                            ins = nc.tensor.matmul(ps[:, b, 0:T], W_LOW[:, j % 2, ws], high[:, k, 0:T],
                                                   start=False, stop=(k == KD - 1))
                        ins.then_inc(filled[b], 1)
            v.end(U_MLP)
            pe.drain().then_inc(pe_stage_end, 1)
            pe.wait_ge(act_stage_end, v.stages)
            pe.wait_ge(dve_stage_end, v.stages)

        def act_mod(act, v, loads=0):
            act.wait_ge(sems["rows_zeroed"], v.of("rows_zeroed"))
            with act.Fori(0, 3) as i:
                for u in range(8):
                    act.wait_ge(filled[u % 4], i * 2 + v.filled(u % 4, u // 4))
                    nc.scalar.activation(ROWS[0:2, u, :], ps[0:2, u % 4, 0:256], ACT.Copy).then_inc(freed[u % 4], 1)
            if loads:
                act.wait_ge(sems["loaded"], loads)
            v.end(U_MOD)
            act.drain().then_inc(act_stage_end, 1)
            act.wait_ge(pe_stage_end, v.stages)
            act.wait_ge(dve_stage_end, v.stages)

        def act_norm(act, v, blk_norm, T, sh, plain=False):
            for k in range(KD):
                nc.scalar.activation(H[:, k, 0:T], X[:, k, 0:T], ACT.Square).then_inc(sems["squares"], 1)
            act.wait_ge(freed[0], v.freed(0))
            nc.scalar.activation(RS[:, 0, 0:T], RS[:, 0, 0:T], ACT.Sqrt).then_inc(sems["root"], 1)
            if not plain:
                for k in range(KD):
                    act.wait_ge(sems["scaled"], v.of("scaled", k + 1))
                    for s in range(T // L):
                        nc.scalar.activation(H[:, k, s * L:(s + 1) * L], H[:, k, s * L:(s + 1) * L], ACT.Identity,
                                             bias=M[:, 2 * (sh + k) + s:2 * (sh + k) + s + 1],
                                             scale=SA[:, blk_norm, 2 * k + s:2 * k + s + 1])
            v.end(U_FNORM if plain else U_NORM)
            act.drain().then_inc(act_stage_end, 1)
            act.wait_ge(pe_stage_end, v.stages)
            act.wait_ge(dve_stage_end, v.stages)

        def act_in(act, v, l):
            T = T2 if l == 0 else L
            for n in range(0, 14, 2):
                b = n % 8
                tok = T2 if n in (4,) else T
                act.wait_ge(filled[b], v.filled(b, n // 8))
                nc.scalar.activation(PX[:, n, 0:tok], ps[:, b, 0:tok], ACT.Copy).then_inc(freed[b], 1)
            v.end(U_IN)
            act.drain().then_inc(act_stage_end, 1)
            act.wait_ge(pe_stage_end, v.stages)
            act.wait_ge(dve_stage_end, v.stages)

        def act_lora(act, v, l):
            T = T2 if l == 0 else L
            for n, (t, tok) in enumerate(((0, T), (1, T), (2, T), (PKV, T2), (PKV + 1, T2))):
                nc.scalar.activation(H[:, n, 0:tok], PX[:, t, 0:tok], ACT.Square).then_inc(sems["squares"], 1)
            for n, tok in enumerate((T, T2)):
                act.wait_ge(freed[n], v.freed(n))
                nc.scalar.activation(RS[:, n, 0:tok], RS[:, n, 0:tok], ACT.Sqrt).then_inc(sems["root"], 1)
            v.end(U_LORA)
            act.drain().then_inc(act_stage_end, 1)
            act.wait_ge(pe_stage_end, v.stages)
            act.wait_ge(dve_stage_end, v.stages)

        def act_up(act, v, l):
            T = T2 if l == 0 else L
            for h in range(0, HEADS, 2):
                act.wait_ge(filled[h], v.filled(h))
                nc.scalar.activation(QT[:, h, 0:T], ps[:, h, 0:T], ACT.Copy).then_inc(freed[h], 1)
            for h in range(0, HEADS, 2):
                act.wait_ge(filled[h], v.filled(h, 1))
                nc.scalar.activation(KT[0:NOPE, h, :], ps[0:NOPE, h, :], ACT.Copy).then_inc(freed[h], 1)
            for t in range(0, NT, 2):
                act.wait_ge(filled[t], v.filled(t, 2))
                nc.scalar.activation(VT[:, t, :], ps[:, t, :], ACT.Copy).then_inc(freed[t], 1)
            v.end(U_UP)
            act.drain().then_inc(act_stage_end, 1)
            act.wait_ge(pe_stage_end, v.stages)
            act.wait_ge(dve_stage_end, v.stages)

        SCALE = float(NOPE + ROPE) ** -0.5

        def act_attn(act, v, l):
            units = attn_units(l)
            n = len(units)
            for i in range(n + 1):
                if i < n:
                    kn = keys_of(units[i][0])[1]
                    b = i % 2
                    act.wait_ge(sems["maxed"], v.of("maxed", i + 1))
                    ins = nc.scalar.activation(PR[:, b, 0:kn], ps[:, b, 0:kn], ACT.Exp, bias=ST[:, 0, i:i + 1], scale=SCALE,
                                               accum_out=ST[:, 1, i:i + 1])
                    ins.then_inc(freed[b], 1)
                if i >= 1:
                    u = i - 1
                    kn = keys_of(units[u][0])[1]
                    b = 2 + u % 2
                    act.wait_ge(filled[b], v.filled(b, u // 2))
                    if u >= 2:
                        act.wait_ge(filled[4 + u % 2], v.filled(4 + u % 2, u // 2 - 1))
                    ins = nc.scalar.activation(PT[:, u % 2, 0:kn], ps[:, b, 0:kn], ACT.Copy)
                    ins.then_inc(freed[b], 1)
            v.end(u_attn(l))
            act.drain().then_inc(act_stage_end, 1)
            act.wait_ge(pe_stage_end, v.stages)
            act.wait_ge(dve_stage_end, v.stages)

        def act_fnet(act, v, l):
            n1 = 2 * seqs(l)
            for t in range(n1):
                act.wait_ge(filled[t], v.filled(t))
                nc.scalar.activation(YF[:, t, :], ps[:, t, :], ACT.Copy).then_inc(freed[t], 1)
            v.end(u_fnet(l))
            act.drain().then_inc(act_stage_end, 1)
            act.wait_ge(pe_stage_end, v.stages)
            act.wait_ge(dve_stage_end, v.stages)

        def act_filter(act, v, l):
            for n in range(2):
                act.wait_ge(sems["reduced"], v.of("reduced", n + 1))
                nc.scalar.activation(SN[0:FILT, 4 + n, :], SN[0:FILT, 1, :], ACT.Sin).then_inc(sems["sines"], 1)
            v.end(u_filter(l))
            act.drain().then_inc(act_stage_end, 1)
            act.wait_ge(pe_stage_end, v.stages)
            act.wait_ge(dve_stage_end, v.stages)

        def act_hyena(act, v, l):
            S = seqs(l)
            for i in range(6):
                w1 = vec("cw", 18 * l + 6 + i)
                nc.scalar.activation(U[:, i, 0:S * L], PX[:, PH + i, 0:S * L], ACT.Identity,
                                              bias=vec("cb", 6 * l + i), scale=w1).then_inc(sems["affine"], 1)
            for f in range(2):
                act.wait_ge(filled[4 + f], v.filled(4 + f))
                nc.scalar.activation(KS[:, f, :], ps[:, 4 + f, :], ACT.Copy).then_inc(freed[4 + f], 1)
            for a in range(2):
                act.wait_ge(filled[6 + a], v.filled(6 + a))
                ins = nc.scalar.activation(ZT[:, a, 0:S * 256], ps[:, 6 + a, 0:S * 256], ACT.Copy).then_inc(freed[6 + a], 1)
            v.end(u_hyena(l))
            act.drain().then_inc(act_stage_end, 1)
            act.wait_ge(pe_stage_end, v.stages)
            act.wait_ge(dve_stage_end, v.stages)

        def act_mlp(act, v, T):
            act.wait_ge(landed[v.place(0)], v.landed(0))
            nc.scalar.activation(W_HIGH[:, 0, :], ring[:, v.place(0)], ACT.Copy).then_inc(sems["w_high"], 1)
            for k in range(KD):
                nc.scalar.activation(H_HIGH[:, k, 0:T], H[:, k, 0:T], ACT.Copy).then_inc(sems["h_high"], 1)

            def quarter(i, more):
                for j in range(8):
                    if j < 7 or more:
                        s, last = v.place(j + 1), 2 * ((j - 1) % 4) + 1
                        act.wait_ge(landed[s], v.landed(j + 1, i, 8))
                        act.wait_ge(filled[last], i * 2 + v.filled(last, (j - 1) // 4))
                        nc.scalar.activation(W_HIGH[:, (j + 1) % 2, :], ring[:, s], ACT.Copy).then_inc(sems["w_high"], 1)
                    for n in ((2 * j, 2 * j + 1) if j < 4 else ()):
                        act.wait_ge(filled[n], i * 2 + v.filled(n))
                        nc.scalar.activation(RELU[:, n % 2, 0:T], ps[:, n, 0:T], ACT.Relu).then_inc(freed[n], 1)
                        for m in ([n - 1] if n else []) + ([n] if n == 7 else []):
                            act.wait_ge(sems["squared"], i * 8 + v.of("squared", m + 1))
                            nc.scalar.activation(HID_HIGH[:, m, 0:T], SQR[:, m % 2, 0:T], ACT.Copy).then_inc(sems["hidden_high"], 1)

            with act.Fori(0, 3) as i:
                quarter(i, True)
            quarter(3, False)
            v.end(U_MLP)
            act.drain().then_inc(act_stage_end, 1)
            act.wait_ge(pe_stage_end, v.stages)
            act.wait_ge(dve_stage_end, v.stages)

        def dve_mod(dve, v, l, bname, g1, g2):
            b0 = VCOL[bname][0] + 2 * MT * l
            nc.vector.memset(ROWS, 0.0).then_inc(sems["rows_zeroed"], 1)
            with dve.Fori(0, 3) as i:
                for u in range(8):
                    b = 4 + u % 4
                    dve.wait_ge(filled[b], i * 2 + v.filled(b, u // 4))
                    turned = ps[:, b, 0:256].rearrange("p (t c) -> p t c", t=2)[:, :, 0:2]
                    nc.vector.tensor_tensor(M[:, bass.ds(i * 32 + 4 * u, 4)].rearrange("p (t c) -> p t c", t=2), turned,
                                            V[:, bass.ds(i * 32 + (b0 + 4 * u), 4)].rearrange("p (t c) -> p t c", t=2),
                                            ALU.add).then_inc(freed[b], 1)
            for n, (g, sc) in enumerate(((g1, 1), (g2, 4))):
                for b in range(4, 8):
                    dve.wait_ge(freed[b], v.freed(b, 6))
                nc.vector.scalar_tensor_tensor(SA[:, n, :], M[:, 16 * sc:16 * sc + 16], 1.0, vec(g, 16 * l, 16), ALU.add, ALU.mult)
            v.end(U_MOD)
            dve.drain().then_inc(dve_stage_end, 1)
            dve.wait_ge(pe_stage_end, v.stages)
            dve.wait_ge(act_stage_end, v.stages)

        def dve_rms(dve, v, b, row, T, width, nth=0, n=1):
            dve.wait_ge(filled[b], v.filled(b, nth))
            nc.vector.tensor_scalar(RS[:, row, 0:T], ps[:, b, 0:T], 1.0 / width, EPS, ALU.mult, ALU.add).then_inc(freed[b], 1)
            dve.wait_ge(sems["root"], v.of("root", n))
            nc.vector.reciprocal(RS[:, row, 0:T], RS[:, row, 0:T]).then_inc(dve_step, v.step())
            dve.wait_ge(dve_step, v.steps())

        def dve_norm(dve, v, T):
            dve_rms(dve, v, 0, 0, T, D)
            for k in range(KD):
                nc.vector.tensor_tensor(H[:, k, 0:T], X[:, k, 0:T], RS[:, 0, 0:T], ALU.mult).then_inc(sems["scaled"], 1)
            v.end(U_NORM)
            dve.drain().then_inc(dve_stage_end, 1)
            dve.wait_ge(pe_stage_end, v.stages)
            dve.wait_ge(act_stage_end, v.stages)

        def dve_final(dve, v):
            dve_rms(dve, v, 0, 0, L, D)
            for k in range(KD):
                nc.vector.scalar_tensor_tensor(X[:, k, 0:L], X[:, k, 0:L], vec("gf", k), RS[:, 0, 0:L], ALU.mult, ALU.mult)
            v.end(U_FNORM)
            dve.drain().then_inc(dve_stage_end, 1)
            dve.wait_ge(pe_stage_end, v.stages)
            dve.wait_ge(act_stage_end, v.stages)

        def pe_final(pe, v):
            pe.wait_ge(freed[0], v.free(0))
            for k in range(KD):
                pe.wait_ge(sems["squares"], v.of("squares", k + 1))
                ins = nc.tensor.matmul(ps[:, 0, 0:L], ones[:], H[:, k, 0:L], start=(k == 0), stop=(k == KD - 1))
            ins.then_inc(filled[0], 1)
            v.end(U_FNORM)
            pe.drain().then_inc(pe_stage_end, 1)
            pe.wait_ge(act_stage_end, v.stages)
            pe.wait_ge(dve_stage_end, v.stages)

        def dve_in(dve, v, l):
            T = T2 if l == 0 else L
            for n in range(1, 14, 2):
                b = n % 8
                tok = T2 if n in (3, 5) else T
                dve.wait_ge(filled[b], v.filled(b, n // 8))
                nc.vector.tensor_copy(PX[:, n, 0:tok], ps[:, b, 0:tok]).then_inc(freed[b], 1)
            v.end(U_IN)
            dve.drain().then_inc(dve_stage_end, 1)
            dve.wait_ge(pe_stage_end, v.stages)
            dve.wait_ge(act_stage_end, v.stages)

        def dve_lora(dve, v, l):
            T = T2 if l == 0 else L
            for n, (t0, nt, tok, g, width) in enumerate(((0, 3, T, "qg", QLORA), (PKV, 2, T2, "kvg", KVLORA))):
                dve_rms(dve, v, n, n, tok, width, n=n + 1)
                for k in range(nt):
                    nc.vector.scalar_tensor_tensor(PX[:, t0 + k, 0:tok], PX[:, t0 + k, 0:tok], vec(g, nt * l + k),
                                                   RS[:, n, 0:tok], ALU.mult, ALU.mult)
            KR = PX[:, PKR, :]
            nc.vector.tensor_tensor(RT[64:96, 0, :], KR[96:128, 0:L], C[96:128, 0:L], ALU.mult).then_inc(dve_step, v.step())
            nc.vector.tensor_tensor(KR[64:96, 0:L], KR[64:96, 0:L], C[64:96, 0:L], ALU.mult).then_inc(dve_step, v.step())
            dve.wait_ge(dve_step, v.steps())
            nc.vector.tensor_tensor(KR[64:96, 0:L], KR[64:96, 0:L], RT[64:96, 0, :], ALU.add)
            v.end(U_LORA)
            dve.drain().then_inc(dve_stage_end, 1)
            dve.wait_ge(pe_stage_end, v.stages)
            dve.wait_ge(act_stage_end, v.stages)

        def dve_up(dve, v, l):
            T = T2 if l == 0 else L
            for h in range(HEADS):
                nc.vector.tensor_copy(KT[64:96, h, :], PX[64:96, PKR, :])
            for h in range(1, HEADS, 2):
                dve.wait_ge(filled[h], v.filled(h))
                nc.vector.tensor_copy(QT[:, h, 0:T], ps[:, h, 0:T]).then_inc(freed[h], 1)
            for h in range(1, HEADS, 2):
                dve.wait_ge(filled[h], v.filled(h, 1))
                nc.vector.tensor_copy(KT[0:NOPE, h, :], ps[0:NOPE, h, :]).then_inc(freed[h], 1)
            for t in range(1, NT, 2):
                dve.wait_ge(filled[t], v.filled(t, 2))
                nc.vector.tensor_copy(VT[:, t, :], ps[:, t, :]).then_inc(freed[t], 1)
            for h in range(HEADS):
                dve.wait_ge(freed[h], v.freed(h))
            for h in range(HEADS):
                nc.vector.tensor_tensor(RT[64:96, h, :], QT[96:128, h, 0:L], C[96:128, 0:L], ALU.mult).then_inc(dve_step, v.step())
                nc.vector.tensor_tensor(QT[64:96, h, 0:L], QT[64:96, h, 0:L], C[64:96, 0:L], ALU.mult).then_inc(dve_step, v.step())
            dve.wait_ge(dve_step, v.steps())
            for h in range(HEADS):
                nc.vector.tensor_tensor(QT[64:96, h, 0:L], QT[64:96, h, 0:L], RT[64:96, h, :], ALU.add)
            v.end(U_UP)
            dve.drain().then_inc(dve_stage_end, 1)
            dve.wait_ge(pe_stage_end, v.stages)
            dve.wait_ge(act_stage_end, v.stages)

        def dve_attn(dve, v, l):
            units = attn_units(l)
            n = len(units)
            for i in range(n + 3):
                if i < n:
                    kn = keys_of(units[i][0])[1]
                    b = i % 2
                    dve.wait_ge(filled[b], v.filled(b, i // 2))
                    nc.vector.reduce_max(ST[:, 2, i:i + 1], ps[:, b, 0:kn], AX.X).then_inc(dve_step, v.step())
                    dve.wait_ge(dve_step, v.steps())
                    if i >= 2:
                        dve.wait_ge(filled[2 + i % 2], v.filled(2 + i % 2, i // 2 - 1))
                    nc.vector.tensor_scalar(ST[:, 0, i:i + 1], ST[:, 2, i:i + 1], -SCALE, None, ALU.mult).then_inc(sems["maxed"], 1)
                    dve.wait_ge(freed[b], v.freed(b, i // 2 + 1))
                    nc.vector.reciprocal(ST[:, 3, i:i + 1], ST[:, 1, i:i + 1]).then_inc(dve_step, v.step())
                    dve.wait_ge(dve_step, v.steps())
                    nc.vector.tensor_scalar(PR[:, b, 0:kn], PR[:, b, 0:kn], ST[:, 3, i:i + 1], None, ALU.mult).then_inc(sems["normed"], 1)
                if i >= 3:
                    u = i - 3
                    s, h, q = units[u]
                    b = 4 + u % 2
                    r = 64 * (h % 2)
                    dve.wait_ge(filled[b], v.filled(b, u // 2))
                    nc.vector.tensor_copy(MIX[r:r + 64, h // 2, s * L + q * P:s * L + (q + 1) * P], ps[r:r + 64, b, 0:P]).then_inc(freed[b], 1)
            v.end(u_attn(l))
            dve.drain().then_inc(dve_stage_end, 1)
            dve.wait_ge(pe_stage_end, v.stages)
            dve.wait_ge(act_stage_end, v.stages)

        def dve_fnet(dve, v, l):
            n1 = 2 * seqs(l)
            for u in range(n1):
                s, f = u // 2, u % 2
                b = (n1 + u) % 8
                dve.wait_ge(filled[b], v.filled(b))
                nc.vector.tensor_copy(MIX[:, 4 + f, s * L:(s + 1) * L], ps[:, b, 0:256]).then_inc(freed[b], 1)
            v.end(u_fnet(l))
            dve.drain().then_inc(dve_stage_end, 1)
            dve.wait_ge(pe_stage_end, v.stages)
            dve.wait_ge(act_stage_end, v.stages)

        def dve_filter(dve, v, l):
            def chain(ins):
                ins.then_inc(dve_step, v.step())
                dve.wait_ge(dve_step, v.steps())

            TWO_PI = 2 * np.pi
            c1 = float(np.float32(6.28125))
            c2 = float(np.float32(TWO_PI - c1))
            c3 = float(TWO_PI - c1 - c2)
            magic = 12582912.0
            for n in range(2):
                dve.wait_ge(filled[n], v.filled(n))
                y, r = SN[0:FILT, 0, :], SN[0:FILT, 1, :]
                turns = SN[0:FILT, 2, :]
                if n:
                    dve.wait_ge(sems["sines"], v.of("sines", 1))
                bias = V[0:FILT, VCOL["hb1" if n == 0 else "hb2"][0] + l:VCOL["hb1" if n == 0 else "hb2"][0] + l + 1]
                fr = V[0:FILT, VCOL["hfreq"][0] + l:VCOL["hfreq"][0] + l + 1]
                nc.vector.tensor_scalar(y, ps[0:FILT, n, 0:L], bias, fr, ALU.add, ALU.mult).then_inc(freed[n], 1)
                dve.wait_ge(freed[n], v.freed(n))
                chain(nc.vector.tensor_scalar(turns, y, 1 / TWO_PI, magic, ALU.mult, ALU.add))
                chain(nc.vector.tensor_scalar(turns, turns, -magic, None, ALU.add))
                chain(nc.vector.scalar_tensor_tensor(r, turns, -c1, y, ALU.mult, ALU.add))
                chain(nc.vector.scalar_tensor_tensor(r, turns, -c2, r, ALU.mult, ALU.add))
                chain(nc.vector.scalar_tensor_tensor(r, turns, -c3, r, ALU.mult, ALU.add))
                nc.vector.tensor_scalar(r, r, 3.1415925, -3.1415925, ALU.min, ALU.max).then_inc(sems["reduced"], 1)
            for a in range(2):
                dve.wait_ge(filled[2 + a], v.filled(2 + a))
                nc.vector.tensor_tensor(HF[:, a, :], ps[:, 2 + a, :], cst("decay", a * 512, a * 512 + 512), ALU.mult).then_inc(freed[2 + a], 1)
            dve.wait_ge(freed[3], v.freed(3))
            for a in range(2):
                nc.vector.tensor_tensor(HS[:, a, 0:256], HF[:, a, 0:256], HF[:, a, 256:512], ALU.add)
                nc.vector.tensor_tensor(HS[:, a, 256:512], HF[:, a, 0:256], HF[:, a, 256:512], ALU.subtract)
                nc.vector.tensor_scalar(YS[:, a, :], HF[:, a, :], -1.0, None, ALU.mult).then_inc(dve_step, v.step())
            dve.wait_ge(dve_step, v.steps())
            for a in range(2):
                nc.vector.tensor_tensor(YS[:, a, :], YS[:, a, :], HF[:, a, :], ALU.max).then_inc(dve_step, v.step())
            dve.wait_ge(dve_step, v.steps())
            for a in range(2):
                ins = nc.vector.tensor_tensor(KA[:, a, :], YS[:, a, 0:256], YS[:, a, 256:512], ALU.add)
            ins.then_inc(sems["decayed"], 1)
            dve.wait_ge(filled[4], v.filled(4))
            nc.vector.reciprocal(RK[:, 0:2], ps[:, 4, 0:2]).then_inc(freed[4], 1)
            v.end(u_filter(l))
            dve.drain().then_inc(dve_stage_end, 1)
            dve.wait_ge(pe_stage_end, v.stages)
            dve.wait_ge(act_stage_end, v.stages)

        def dve_hyena(dve, v, l):
            S = seqs(l)

            def seq(ap, a, b):
                return ap.rearrange("p (s t) -> p s t", t=L)[:, 0:S, a:b]

            for tap, (da, db, sa, s_b) in ((0, (1, L, 0, L - 1)), (2, (0, L - 1, 1, L))):
                for i in range(6):
                    if tap == 0:
                        dve.wait_ge(sems["affine"], v.of("affine", i + 1))
                    nc.vector.scalar_tensor_tensor(seq(U[:, i, :], da, db), seq(PX[:, PH + i, :], sa, s_b),
                                                          vec("cw", 18 * l + 6 * tap + i), seq(U[:, i, :], da, db), ALU.mult, ALU.add).then_inc(dve_step, v.step())
                dve.wait_ge(dve_step, v.steps())
            for c in range(2):
                ins = nc.vector.tensor_tensor(Z[:, c, 0:S * L], U[:, 2 + c, 0:S * L], U[:, 4 + c, 0:S * L], ALU.mult)
            ins.then_inc(sems["zmul"], 1)
            dve.wait_ge(sems["zmul"], v.of("zmul", 1))
            for f in range(2):
                dve.wait_ge(freed[4 + f], v.freed(4 + f))
            for f in range(2):
                for r in range(2):
                    b = 2 * f + r
                    dve.wait_ge(filled[b], v.filled(b))
                    for q in range(2):
                        kk = KS[:, f, q * 256:(q + 1) * 256].rearrange("p (s c) -> p s c", s=1).broadcast_to([P, S, 256])
                        ins = nc.vector.tensor_tensor(ZS[:, 2 * r + q, 0:S * 256].rearrange("p (s c) -> p s c", c=256),
                                                      ps[:, b, 0:S * 256].rearrange("p (s c) -> p s c", c=256), kk, ALU.mult)
                    ins.then_inc(freed[b], 1)
                dve.wait_ge(freed[2 * f + 1], v.freed(2 * f + 1))
                nc.vector.tensor_tensor(YS[:, 2 * f, 0:S * 256], ZS[:, 0, 0:S * 256], ZS[:, 3, 0:S * 256], ALU.subtract)
                ins = nc.vector.tensor_tensor(YS[:, 2 * f + 1, 0:S * 256], ZS[:, 1, 0:S * 256], ZS[:, 2, 0:S * 256], ALU.add)
                if f == 0:
                    ins.then_inc(dve_step, v.step())
                    dve.wait_ge(dve_step, v.steps())
            ins.then_inc(sems["prod"], 1)
            for u in range(2 * S):
                c, s = u % 2, u // 2
                dve.wait_ge(filled[u], v.filled(u, 1))
                y = ZS[:, u, 0:256]
                nc.vector.tensor_scalar(y, ps[:, u, 0:256], RK[:, c:c + 1], None, ALU.mult).then_inc(freed[u], 1)
                dve.wait_ge(freed[u], v.freed(u, 2))
                nc.vector.scalar_tensor_tensor(y, Z[:, c, s * L:(s + 1) * L], vec("hyd", 2 * l + c), y, ALU.mult, ALU.add).then_inc(dve_step, v.step())
                dve.wait_ge(dve_step, v.steps())
                nc.vector.tensor_tensor(MIX[:, 6 + c, s * L:(s + 1) * L], y, U[:, c, s * L:(s + 1) * L], ALU.mult)
            v.end(u_hyena(l))
            dve.drain().then_inc(dve_stage_end, 1)
            dve.wait_ge(pe_stage_end, v.stages)
            dve.wait_ge(act_stage_end, v.stages)

        def dve_residual(dve, v, n, b, T, gate, nth=0):
            for s in range(T // L):
                ins = nc.vector.scalar_tensor_tensor(X[:, n, s * L:(s + 1) * L], ps[:, b, s * L:(s + 1) * L],
                                                     M[:, 2 * (gate * KD + n) + s:2 * (gate * KD + n) + s + 1],
                                                     X[:, n, s * L:(s + 1) * L], ALU.mult, ALU.add)
            ins.then_inc(freed[b], 1)

        def dve_out(dve, v, T, uses):
            for n in range(KD):
                dve.wait_ge(filled[n], v.filled(n))
                dve_residual(dve, v, n, n, T, 2)
            v.end(uses)
            dve.drain().then_inc(dve_stage_end, 1)
            dve.wait_ge(pe_stage_end, v.stages)
            dve.wait_ge(act_stage_end, v.stages)

        def dve_mlp(dve, v, T):
            dve.wait_ge(sems["w_high"], v.of("w_high"))
            nc.vector.tensor_tensor(W_LOW[:, 0, :], ring[:, v.place(0)], W_HIGH[:, 0, :].bitcast(F32),
                                    ALU.subtract).then_inc(sems["w_split"], 1)
            for k in range(KD):
                dve.wait_ge(sems["h_high"], v.of("h_high", k + 1))
                nc.vector.tensor_tensor(H_LOW[:, k, 0:T], H[:, k, 0:T], H_HIGH[:, k, 0:T].bitcast(F32),
                                        ALU.subtract).then_inc(sems["h_split"], 1)

            def quarter(i, more):
                for j in range(8):
                    if j < 7 or more:
                        dve.wait_ge(sems["w_high"], i * 8 + v.of("w_high", j + 2))
                        nc.vector.tensor_tensor(W_LOW[:, (j + 1) % 2, :], ring[:, v.place(j + 1)],
                                                W_HIGH[:, (j + 1) % 2, :].bitcast(F32), ALU.subtract).then_inc(sems["w_split"], 1)
                    for n in ((2 * j, 2 * j + 1) if j < 4 else ()):
                        dve.wait_ge(freed[n], i * 2 + v.freed(n))
                        if n > 1:
                            dve.wait_ge(sems["hidden_split"], i * 8 + v.of("hidden_split", n - 1))
                        r = RELU[:, n % 2, 0:T]
                        nc.vector.tensor_tensor(SQR[:, n % 2, 0:T], r, r, ALU.mult).then_inc(sems["squared"], 1)
                        for m in ([n - 1] if n else []) + ([n] if n == 7 else []):
                            dve.wait_ge(sems["hidden_high"], i * 8 + v.of("hidden_high", m + 1))
                            nc.vector.tensor_tensor(HID_LOW[:, m, 0:T], SQR[:, m % 2, 0:T], HID_HIGH[:, m, 0:T].bitcast(F32),
                                                    ALU.subtract).then_inc(sems["hidden_split"], 1)
                    for n in ((2 * j - 8, 2 * j - 7) if j > 3 else ()):
                        dve.wait_ge(filled[n], i * 2 + v.filled(n, 1))
                        dve_residual(dve, v, n, n, T, 5)

            with dve.Fori(0, 3) as i:
                quarter(i, True)
            quarter(3, False)
            v.end(U_MLP)
            dve.drain().then_inc(dve_stage_end, 1)
            dve.wait_ge(pe_stage_end, v.stages)
            dve.wait_ge(act_stage_end, v.stages)


        U_CONV_BODY = {**{b: 1 for b in range(8)}, "slab": 4, "convolved": 8, "silu": 8}
        U_L2 = {**banks(16), "squares": 16, "scaled": 17}
        U_VT = banks(16)
        U_GATES = {0: 2, 1: 1, 2: 1, 3: 1, "slab": 1, "abs": 1, "gates": 3}
        U_UNITS = {0: 10, 1: 2, 2: 8, 3: 6, 4: 10, 5: 2, 6: 8, 7: 6, "eye0": 2, "eye1": 2,
                   "gt0": 1, "gt1": 1, "kq0": 2, "kq1": 2, "pt0": 1, "pt1": 1, "ti0": 1, "ti1": 1}
        U_Z = {**banks(16), "slab": 8}
        U_READ = {**banks(16), "sq": 16, "squares": 16, "scales": 2, "scaled": 16}
        U_DOUT = {**banks(8), "slab": 8}
        DIRS = (0, 1)

        def halves(d):
            return ((2, 1), (0, 1)) if d == 0 else ((3, -1), (1, -1))

        def chunk(first, step, st):
            return st * step + first

        def pe_conv(pe, v):
            with pe.Fori(0, 4) as i, v.loop(i, 4, U_CONV_BODY):
                for u in range(4):
                    pe.wait_ge(landed[(v.base.get('slab', 0) + u) % RING], i * 16 + 16 * ((v.base.get("slab", 0) + u) // RING + 1))
                    w = slab_view((v.base.get("slab", 0) + u) % RING, KD, 256)
                    for t in range(2):
                        b = 2 * u + t
                        pe.wait_ge(freed[b], v.free(b))
                        for k in range(KD):
                            ins = nc.tensor.matmul(ps[:, b, :], w[:, k, t * P:(t + 1) * P], H[:, k, :], start=(k == 0), stop=(k == KD - 1))
                            if t == 0 and k == 0:
                                ins.then_inc(sems["slab_begun"], 1)
                        ins.then_inc(filled[b], 1)
            v.end({"gates": 1})
            pe.drain().then_inc(pe_stage_end, 1)
            pe.wait_ge(act_stage_end, v.stages)
            pe.wait_ge(dve_stage_end, v.stages)

        def act_conv(act, v):
            act.wait_ge(sems["gates"], v.of("gates", 1))
            with act.Fori(0, 4) as i, v.loop(i, 4, U_CONV_BODY):
                for n in range(10):
                    if n < 8:
                        act.wait_ge(filled[n], v.filled(n))
                        if n >= 4:
                            act.wait_ge(sems["convolved"], v.of("convolved", n - 3))
                        nc.scalar.activation(CB[:, n % 4, :].rearrange("p (s t) -> p s t", s=2)[:, :, 2:2 + L],
                                                     ps[:, n, :].rearrange("p (s t) -> p s t", s=2), ACT.Copy).then_inc(freed[n], 1)
                    if n >= 2:
                        act.wait_ge(sems["convolved"], v.of("convolved", n - 1))
                        nc.scalar.activation(QKV[:, i * 8 + (n - 2), :], CO[:, (n - 2) % 4, :], ACT.Silu).then_inc(sems["silu"], 1)
            v.end({"gates": 1})
            act.drain().then_inc(act_stage_end, 1)
            act.wait_ge(pe_stage_end, v.stages)
            act.wait_ge(dve_stage_end, v.stages)

        def dve_conv(dve, v):
            nc.vector.memset(CB[:, :, :], 0.0).then_inc(sems["gates"], 1)
            at = VCOL["dncw"][0]
            with dve.Fori(0, 4) as i, v.loop(i, 4, {**U_CONV_BODY, "dve_step": 32}):
                for n in range(8):
                    dve.wait_ge(freed[n], v.freed(n))
                    dve.wait_ge(sems["silu"], v.of("silu", max(0, n - 3)))
                    row = CB[:, n % 4, :].rearrange("p (s t) -> p s t", s=2)
                    o = CO[:, n % 4, :].rearrange("p (s t) -> p s t", s=2)
                    nc.vector.tensor_scalar(o, row[:, :, 0:L], V[:, bass.ds(i * 40 + (at + 5 * n), 1)], None, ALU.mult).then_inc(dve_step, v.step())
                    for tap in range(1, 5):
                        dve.wait_ge(dve_step, v.steps())
                        ins = nc.vector.scalar_tensor_tensor(o, row[:, :, tap:tap + L], V[:, bass.ds(i * 40 + (at + 5 * n + tap), 1)],
                                                             o, ALU.mult, ALU.add)
                        if tap < 4:
                            ins.then_inc(dve_step, v.step())
                    ins.then_inc(sems["convolved"], 1)
            v.end({"gates": 1})
            dve.drain().then_inc(dve_stage_end, 1)
            dve.wait_ge(pe_stage_end, v.stages)
            dve.wait_ge(act_stage_end, v.stages)

        def pe_l2(pe, v):
            for t in range(16):
                b = t % 8
                pe.wait_ge(sems["squares"], v.of("squares", t + 1))
                pe.wait_ge(freed[b], v.free(b, t // 8))
                nc.tensor.matmul(ps[:, b, :], ones[:], SQ[:, t % 2, :], start=True, stop=True).then_inc(filled[b], 1)
            v.end(U_L2)
            pe.drain().then_inc(pe_stage_end, 1)
            pe.wait_ge(act_stage_end, v.stages)
            pe.wait_ge(dve_stage_end, v.stages)

        def act_l2(act, v):
            for i in range(17):
                if i < 16:
                    if i >= 2:
                        act.wait_ge(filled[(i - 2) % 8], v.filled((i - 2) % 8, (i - 2) // 8))
                    nc.scalar.activation(SQ[:, i % 2, :], QK[:, i, :], ACT.Square).then_inc(sems["squares"], 1)
                if i >= 1:
                    t = i - 1
                    act.wait_ge(sems["scaled"], v.of("scaled", max(t - 2, 1)))
                    act.wait_ge(filled[t % 8], v.filled(t % 8, t // 8))
                    nc.scalar.activation(RR[:, t % 4, :], ps[:, t % 8, :], ACT.Sqrt, bias=MS[:, 63:64]).then_inc(freed[t % 8], 1)
            v.end(U_L2)
            act.drain().then_inc(act_stage_end, 1)
            act.wait_ge(pe_stage_end, v.stages)
            act.wait_ge(dve_stage_end, v.stages)

        def dve_l2(dve, v):
            nc.vector.memset(MS[:, 63:64], EPS).then_inc(sems["scaled"], 1)
            for t in range(16):
                dve.wait_ge(freed[t % 8], v.freed(t % 8, t // 8 + 1))
                nc.vector.reciprocal(RR[:, t % 4, :], RR[:, t % 4, :]).then_inc(dve_step, v.step())
                dve.wait_ge(dve_step, v.steps())
                nc.vector.scalar_tensor_tensor(QK[:, t, :], QK[:, t, :], float(P) ** -0.5 if t < 8 else 1.0,
                                               RR[:, t % 4, :], ALU.mult, ALU.mult).then_inc(sems["scaled"], 1)
            v.end(U_L2)
            dve.drain().then_inc(dve_stage_end, 1)
            dve.wait_ge(pe_stage_end, v.stages)
            dve.wait_ge(act_stage_end, v.stages)

        def pe_vt(pe, v):
            for h in range(DNH):
                b = h % 8
                pe.wait_ge(freed[b], v.free(b, h // 8))
                for t in range(NT):
                    ins = nc.tensor.transpose(ps[:, b, t * P:(t + 1) * P], VV[:, h, t * P:(t + 1) * P], ident[:])
                ins.then_inc(filled[b], 1)
            v.end(U_VT)
            pe.drain().then_inc(pe_stage_end, 1)
            pe.wait_ge(act_stage_end, v.stages)
            pe.wait_ge(dve_stage_end, v.stages)

        def act_vt(act, v):
            for h in range(0, DNH, 2):
                act.wait_ge(filled[h % 8], v.filled(h % 8, h // 8))
                nc.scalar.activation(VV[:, h, :], ps[:, h % 8, :], ACT.Copy).then_inc(freed[h % 8], 1)
            v.end(U_VT)
            act.drain().then_inc(act_stage_end, 1)
            act.wait_ge(pe_stage_end, v.stages)
            act.wait_ge(dve_stage_end, v.stages)

        def dve_vt(dve, v):
            for h in range(1, DNH, 2):
                dve.wait_ge(filled[h % 8], v.filled(h % 8, h // 8))
                nc.vector.tensor_copy(VV[:, h, :], ps[:, h % 8, :]).then_inc(freed[h % 8], 1)
            v.end(U_VT)
            dve.drain().then_inc(dve_stage_end, 1)
            dve.wait_ge(pe_stage_end, v.stages)
            dve.wait_ge(act_stage_end, v.stages)

        def sc4(kind):
            return SC[:, kind, :].rearrange("p (t c) -> p t c", t=NT)

        def pe_gates(pe, v):
            s = v.place(0)
            pe.wait_ge(landed[s], v.landed(0))
            w = slab_view(s, KD, 256)
            for t in range(NT):
                pe.wait_ge(freed[t], v.free(t))
                for k in range(KD):
                    ins = nc.tensor.matmul(ps[:, t, 0:64], H[:, k, t * P:(t + 1) * P], w[:, k, 0:64], start=(k == 0), stop=(k == KD - 1))
                    if t == 0 and k == 0:
                        ins.then_inc(sems["slab_begun"], 1)
                ins.then_inc(filled[t], 1)
            pe.wait_ge(sems["gates"], v.of("gates", 2))
            pe.wait_ge(freed[0], v.free(0, 1))
            for kind in range(3):
                for d in DIRS:
                    lhs = [cst("incl", d * P, d * P + P), cst("after", d * P, d * P + P), ones[:]][kind]
                    ins = nc.tensor.matmul(ps[:, 0, (kind * 2 + d) * 64:(kind * 2 + d) * 64 + 64], lhs,
                                           sc4(SG_)[:, :, d * 16:d * 16 + 16], start=True, stop=True)
            ins.then_inc(filled[0], 1)
            v.end(U_GATES)
            pe.drain().then_inc(pe_stage_end, 1)
            pe.wait_ge(act_stage_end, v.stages)
            pe.wait_ge(dve_stage_end, v.stages)

        def act_gates(act, v):
            for t in range(NT):
                act.wait_ge(freed[t], v.freed(t))
                nc.scalar.activation(sc4(SB_)[:, t, :], sc4(SB_)[:, t, :], ACT.Sigmoid).then_inc(act_step, v.step())
            act.wait_ge(sems["abs"], v.of("abs", 1))
            nc.scalar.activation(TG[:, 1, :], TG[:, 1, :], ACT.Exp, scale=-1.0).then_inc(act_step, v.step())
            nc.scalar.activation(TG[:, 2, 0:32], vec("alog", 0, 32), ACT.Exp)
            act.wait_ge(act_step, v.steps())
            nc.scalar.activation(TG[:, 1, :], TG[:, 1, :], ACT.Ln, bias=ones[:, 0:1]).then_inc(sems["gates"], 1)
            act.wait_ge(filled[0], v.filled(0, 1))
            for kind, dst in ((0, SEG), (1, SBT), (2, SET)):
                for d in DIRS:
                    ins = nc.scalar.activation(sc4(dst)[:, :, d * 16:d * 16 + 16],
                                               ps[:, 0, (kind * 2 + d) * 64:(kind * 2 + d) * 64 + 64].rearrange("p (t c) -> p t c", t=NT), ACT.Exp)
            ins.then_inc(freed[0], 1)
            v.end(U_GATES)
            act.drain().then_inc(act_stage_end, 1)
            act.wait_ge(pe_stage_end, v.stages)
            act.wait_ge(dve_stage_end, v.stages)

        def dve_gates(dve, v):
            x = TG[:, 0, :].rearrange("p (t c) -> p t c", t=NT)
            for t in range(NT):
                dve.wait_ge(filled[t], v.filled(t))
                nc.vector.tensor_tensor(x[:, t, :], ps[:, t, 0:32], vec("dt", 0, 32), ALU.add).then_inc(dve_step, v.step())
                nc.vector.tensor_copy(sc4(SB_)[:, t, :], ps[:, t, 32:64]).then_inc(freed[t], 1)
            dve.wait_ge(dve_step, v.steps())
            nc.vector.scalar_tensor_tensor(TG[:, 1, :], TG[:, 0, :], -1.0, TG[:, 0, :], ALU.mult, ALU.max).then_inc(sems["abs"], 1)
            dve.wait_ge(sems["gates"], v.of("gates", 1))
            nc.vector.scalar_tensor_tensor(TG[:, 0, :], TG[:, 0, :], 0.0, TG[:, 1, :], ALU.max, ALU.add).then_inc(dve_step, v.step())
            dve.wait_ge(dve_step, v.steps())
            for t in range(NT):
                ins = nc.vector.scalar_tensor_tensor(sc4(SG_)[:, t, :], x[:, t, :], -1.0, TG[:, 2, 0:32], ALU.mult, ALU.mult)
            ins.then_inc(sems["gates"], 1)
            dve.wait_ge(freed[0], v.freed(0, 2))
            nc.vector.tensor_scalar(SC[:, SNB, :], SC[:, SB_, :], -1.0, None, ALU.mult)
            nc.vector.tensor_scalar(SC[:, SNEG, :], SC[:, SEG, :], -1.0, None, ALU.mult)
            nc.vector.tensor_tensor(SC[:, SBT, :], SC[:, SBT, :], SC[:, SB_, :], ALU.mult).then_inc(sems["gates"], 1)
            v.end(U_GATES)
            dve.drain().then_inc(dve_stage_end, 1)
            dve.wait_ge(pe_stage_end, v.stages)
            dve.wait_ge(act_stage_end, v.stages)

        def unit(u, buf):
            return UB[u][:, buf, :]

        def heads4(ap):
            return ap.rearrange("p (h n) -> p h n", h=4)

        def level(name, n):
            at = CCOL[name][0] + (n + 1) * P
            return C[:, at:at + P].bitcast(I32).rearrange("p (o n) -> p o n", o=1).broadcast_to([P, 4, P])

        def meet(eng, v):
            v.end({})
            if v.own != "pool":
                eng.drain().then_inc(sems[v.own + "_stage_end"], 1)
            for e in ("pe", "act", "dve"):
                if e != v.own:
                    eng.wait_ge(sems[e + "_stage_end"], v.stages)

        def delta(v, eng, body, own=None):
            for d in DIRS:
                if own == "dve":
                    nc.vector.memset(SS[:, :, :], 0.0)
                meet(eng, v)
                for first, step in halves(d):
                    with eng.Fori(0, 2) as st:
                        with eng.Fori(0, 2) as hp:
                            with v.loop(st * 2 + hp, 4, {**U_UNITS, **({own + "_step": STEPS[own]} if own in STEPS else {})}):
                                body(d, chunk(first, step, st), hp)
                meet(eng, v)

        STEPS = {"dve": 2}

        def plain_wait(n):
            nc.vector.memset(TG[:, 0, n:n + 1], 0.0)

        def pool_delta(pool, v):
            def body(d, c, hp):
                for u in range(2):
                    pool.wait_ge(filled[4 * u + 1], v[4 * u + 1])
                    pool.wait_ge(filled[4 * u + 2], v[4 * u + 2])
                    pool.wait_ge(filled[4 * u + 3], v[4 * u + 3])
                    kq = unit(u, KQ).rearrange("p (h n) -> p h n", h=2)
                    for part_, t0 in ((0, 8), (1, 0)):
                        ins = nc.gpsimd.tensor_copy(kq[:, :, part_ * P:(part_ + 1) * P],
                                                    QK[:, bass.ds(hp * 4 + (t0 + 2 * u), 2), bass.ds(c * P, P)])
                        ins.then_inc(sems[f"kq{u}"], 1)
                    eye = ident[:].rearrange("p (o n) -> p o n", o=1).broadcast_to([P, 4, P])
                    nc.gpsimd.tensor_copy(heads4(unit(u, TT)), eye).then_inc(sems[f"eye{u}"], 1)
                    nc.gpsimd.tensor_copy(heads4(unit(u, TM)), eye).then_inc(sems[f"eye{u}"], 1)
            delta(v, pool, body)

        def pe_delta(pe, v):
            def body(d, c, hp):
                two = range(2)
                for u in two:
                    a = 4 * u
                    pe.wait_ge(sems[f"gt{u}"], v.of(f"gt{u}"))
                    pe.wait_ge(freed[a], v.free(a, 0))
                    nc.tensor.matmul(ps[:, a, :], cst("after", d * P, d * P + P), unit(u, GT), start=True, stop=True).then_inc(filled[a], 1)
                for u in two:
                    kq = unit(u, KQ).rearrange("p (h n) -> p h n", h=2)
                    pe.wait_ge(sems[f"kq{u}"], v.of(f"kq{u}", 2))
                    pe.wait_ge(freed[4 * u + 1], v.free(4 * u + 1, 0))
                    for h in range(2):
                        ins = nc.tensor.matmul(ps[:, 4 * u + 1, h * 256:(h + 1) * 256], kq[:, h, 0:P], kq[:, h, :], start=True, stop=True)
                    ins.then_inc(filled[4 * u + 1], 1)
                    pe.wait_ge(freed[4 * u + 2], v.free(4 * u + 2, 0))
                    for h in range(2):
                        ins = nc.tensor.transpose(ps[:, 4 * u + 2, h * P:(h + 1) * P], kq[:, h, 0:P], ident[:])
                    ins.then_inc(filled[4 * u + 2], 1)
                for u in two:
                    pe.wait_ge(sems[f"pt{u}"], v.of(f"pt{u}"))
                    pe.wait_ge(freed[4 * u], v.free(4 * u, 1))
                    for h in range(4):
                        ins = nc.tensor.transpose(ps[:, 4 * u, h * P:(h + 1) * P], unit(u, PTT)[:, h * P:(h + 1) * P], ident[:])
                    ins.then_inc(filled[4 * u], 1)
                for n in range(1, LEV):
                    for u in two:
                        if n == 1:
                            pe.wait_ge(sems[f"ti{u}"], v.of(f"ti{u}"))
                        else:
                            pe.wait_ge(freed[4 * u + 3], v.freed(4 * u + 3, n - 1))
                        pe.wait_ge(freed[4 * u], v.free(4 * u, n + 1))
                        for h in range(4):
                            hs = slice(h * P, (h + 1) * P)
                            ins = nc.tensor.matmul(ps[:, 4 * u, hs], unit(u, PTT)[:, hs], unit(u, TM)[:, hs], start=True, stop=True)
                        ins.then_inc(filled[4 * u], 1)
                    for u in two:
                        pe.wait_ge(freed[4 * u], v.freed(4 * u, n + 2))
                        pe.wait_ge(freed[4 * u + 2], v.free(4 * u + 2, n))
                        for h in range(4):
                            hs = slice(h * P, (h + 1) * P)
                            ins = nc.tensor.matmul(ps[:, 4 * u + 2, hs], unit(u, ZM)[:, hs], unit(u, TT)[:, hs], start=True, stop=True)
                        ins.then_inc(filled[4 * u + 2], 1)
                    if n < LEV - 1:
                        for u in two:
                            pe.wait_ge(freed[4 * u + 2], v.freed(4 * u + 2, n + 1))
                            pe.wait_ge(freed[4 * u + 3], v.free(4 * u + 3, n - 1))
                            for h in range(4):
                                hs = slice(h * P, (h + 1) * P)
                                ins = nc.tensor.transpose(ps[:, 4 * u + 3, hs], unit(u, TT)[:, hs], ident[:])
                            ins.then_inc(filled[4 * u + 3], 1)
                for u in two:
                    kq = unit(u, KQ).rearrange("p (h n) -> p h n", h=2)
                    pe.wait_ge(freed[4 * u], v.free(4 * u, 8))
                    for g, b in ((0, 4 * u), (1, 4 * u + 1)):
                        if g:
                            pe.wait_ge(freed[b], v.free(b, 1))
                        for h in range(2):
                            S = SS[:, bass.ds(hp * 8 + (4 * u + 2 * h), 2), :]
                            ins = nc.tensor.matmul(ps[:, b, h * 256:(h + 1) * 256], kq[:, h, g * P:(g + 1) * P], S, start=True, stop=True)
                        ins.then_inc(filled[b], 1)
                for u in two:
                    pe.wait_ge(freed[4 * u], v.freed(4 * u, 9))
                    pe.wait_ge(freed[4 * u + 2], v.free(4 * u + 2, 7))
                    for h in range(4):
                        hs = slice(h * P, (h + 1) * P)
                        ins = nc.tensor.matmul(ps[:, 4 * u + 2, hs], unit(u, TT)[:, hs], unit(u, ZM)[:, hs], start=True, stop=True)
                    ins.then_inc(filled[4 * u + 2], 1)
                for u in two:
                    pe.wait_ge(freed[4 * u + 2], v.freed(4 * u + 2, 8))
                    pe.wait_ge(freed[4 * u + 3], v.free(4 * u + 3, 5))
                    for h in range(4):
                        hs = slice(h * P, (h + 1) * P)
                        ins = nc.tensor.matmul(ps[:, 4 * u + 3, hs], unit(u, AM)[:, hs], unit(u, TM)[:, hs], start=True, stop=True)
                    ins.then_inc(filled[4 * u + 3], 1)
                    pe.wait_ge(freed[4 * u], v.free(4 * u, 9))
                    for h in range(2):
                        ins = nc.tensor.matmul(ps[:, 4 * u, h * 256:(h + 1) * 256], KTOK[:, u, h * P:(h + 1) * P],
                                               unit(u, DT)[:, h * 256:(h + 1) * 256], start=True, stop=True)
                    ins.then_inc(filled[4 * u], 1)
            delta(v, pe, body)

        def col(kind, d, c, hp, u, h):
            return SC[:, kind, bass.ds(c * 32 + hp * 8 + (16 * d + 4 * u + h), 1)]

        def act_delta(act, v):
            def body(d, c, hp):
                two = range(2)
                for u in two:
                    act.wait_ge(filled[4 * u], v.filled(4 * u, 0))
                    nc.scalar.activation(unit(u, DT), ps[:, 4 * u, :], ACT.Exp).then_inc(freed[4 * u], 1)
                for u in two:
                    act.wait_ge(filled[4 * u + 2], v.filled(4 * u + 2, 0))
                    nc.scalar.activation(KTOK[:, u, :], ps[:, 4 * u + 2, 0:256], ACT.Copy).then_inc(freed[4 * u + 2], 1)
                for n in range(1, LEV):
                    for u in two:
                        act.wait_ge(filled[4 * u], v.filled(4 * u, n + 1))
                        nc.scalar.activation(unit(u, ZM), ps[:, 4 * u, :], ACT.Copy).then_inc(freed[4 * u], 1)
                    if n < LEV - 1:
                        for u in two:
                            act.wait_ge(filled[4 * u + 3], v.filled(4 * u + 3, n - 1))
                            nc.scalar.activation(unit(u, TM), ps[:, 4 * u + 3, :], ACT.Copy).then_inc(freed[4 * u + 3], 1)
                for u in two:
                    act.wait_ge(filled[4 * u + 2], v.filled(4 * u + 2, 7))
                    for dst, kind in ((TM, SB_), (DT, SBT)):
                        for h in range(4):
                            hs = slice(h * P, (h + 1) * P)
                            ins = nc.scalar.activation(unit(u, dst)[:, hs], ps[:, 4 * u + 2, hs], ACT.Copy, scale=col(kind, d, c, hp, u, h))
                    ins.then_inc(freed[4 * u + 2], 1)
            delta(v, act, body)

        def dve_delta(dve, v):
            def body(d, c, hp):
                two = range(2)
                incl = cst("incl", d * P, d * P + P)
                tmask, ttmask = (("lower", "upper"), ("upper", "lower"))[d]
                for u in two:
                    for h in range(4):
                        ins = nc.vector.tensor_scalar(unit(u, GT)[:, h * P:(h + 1) * P], incl, col(SG_, d, c, hp, u, h), None, ALU.mult)
                    ins.then_inc(sems[f"gt{u}"], 1)
                for u in two:
                    dve.wait_ge(freed[4 * u], v.freed(4 * u))
                    dve.wait_ge(filled[4 * u + 1], v.filled(4 * u + 1, 0))
                    dve.wait_ge(filled[4 * u + 3], v[4 * u + 3])
                    qk = ps[:, 4 * u + 1, :].rearrange("p (h n) -> p h n", h=2)
                    for h in range(4):
                        hs = slice(h * P, (h + 1) * P)
                        ins = nc.vector.scalar_tensor_tensor(unit(u, PTT)[:, hs], qk[:, h // 2, 0:P], col(SNB, d, c, hp, u, h),
                                                             unit(u, DT)[:, hs], ALU.mult, ALU.mult)
                    ins.then_inc(sems[f"pt{u}"], 1)
                for u in two:
                    dve.wait_ge(sems[f"eye{u}"], v.of(f"eye{u}", 2))
                    dve.wait_ge(filled[4 * u], v.filled(4 * u, 1))
                    plain_wait(u)
                    nc.vector.copy_predicated(heads4(unit(u, TM)), level(tmask, 0), heads4(ps[:, 4 * u, :])).then_inc(freed[4 * u], 1)
                    nc.vector.copy_predicated(heads4(unit(u, TT)), level(ttmask, 0), heads4(unit(u, PTT))).then_inc(sems[f"ti{u}"], 1)
                for u in two:
                    qk = ps[:, 4 * u + 1, :].rearrange("p (h n) -> p h n", h=2)
                    nc.vector.tensor_tensor(heads4(unit(u, GT)), heads4(unit(u, DT)),
                                                   incl.rearrange("p (o n) -> p o n", o=1).broadcast_to([P, 4, P]), ALU.mult).then_inc(dve_step, v.step())
                    dve.wait_ge(dve_step, v.steps())
                    for h in range(2):
                        ins = nc.vector.tensor_tensor(unit(u, AM)[:, h * 256:(h + 1) * 256].rearrange("p (r n) -> p r n", r=2),
                                                      qk[:, h:h + 1, P:2 * P].broadcast_to([P, 2, P]),
                                                      unit(u, GT)[:, h * 256:(h + 1) * 256].rearrange("p (r n) -> p r n", r=2), ALU.mult)
                    ins.then_inc(freed[4 * u + 1], 1)
                for n in range(1, LEV):
                    for u in two:
                        dve.wait_ge(filled[4 * u + 2], v.filled(4 * u + 2, n))
                        plain_wait(2 * n + u)
                        nc.vector.copy_predicated(heads4(unit(u, TT)), level(ttmask, n), heads4(ps[:, 4 * u + 2, :])).then_inc(freed[4 * u + 2], 1)
                for u in two:
                    dve.wait_ge(filled[4 * u], v.filled(4 * u, 8))
                    for h in range(4):
                        hs = slice(h * P, (h + 1) * P)
                        vv = VV[:, bass.ds(hp * 8 + (4 * u + h), 1), bass.ds(c * P, P)].rearrange("p a b -> p (a b)")
                        ins = nc.vector.scalar_tensor_tensor(unit(u, ZM)[:, hs], ps[:, 4 * u, hs], col(SNEG, d, c, hp, u, h), vv, ALU.mult, ALU.add)
                    ins.then_inc(freed[4 * u], 1)
                for u in two:
                    dve.wait_ge(filled[4 * u + 1], v.filled(4 * u + 1, 1))
                    for h in range(4):
                        hs = slice(h * P, (h + 1) * P)
                        oo = OO[:, bass.ds(hp * 8 + (4 * u + h), 1), bass.ds(c * P, P)].rearrange("p a b -> p (a b)")
                        if d == 0:
                            ins = nc.vector.tensor_scalar(oo, ps[:, 4 * u + 1, hs], col(SEG, d, c, hp, u, h), None, ALU.mult)
                        else:
                            ins = nc.vector.scalar_tensor_tensor(oo, ps[:, 4 * u + 1, hs], col(SEG, d, c, hp, u, h), oo, ALU.mult, ALU.add)
                    ins.then_inc(freed[4 * u + 1], 1)
                    dve.wait_ge(freed[4 * u + 1], v.freed(4 * u + 1, 2))
                    dve.wait_ge(filled[4 * u + 3], v.filled(4 * u + 3, 5))
                    oo = OO[:, bass.ds(hp * 8 + 4 * u, 4), bass.ds(c * P, P)]
                    nc.vector.tensor_tensor(oo, heads4(ps[:, 4 * u + 3, :]), oo, ALU.add).then_inc(freed[4 * u + 3], 1)
                    dve.wait_ge(filled[4 * u], v.filled(4 * u, 9))
                    for h in range(4):
                        hs = slice(h * P, (h + 1) * P)
                        S = SS[:, bass.ds(hp * 8 + (4 * u + h), 1), :].rearrange("p a b -> p (a b)")
                        ins = nc.vector.scalar_tensor_tensor(S, S, col(SET, d, c, hp, u, h), ps[:, 4 * u, hs], ALU.mult, ALU.add)
                    ins.then_inc(freed[4 * u], 1)
            delta(v, dve, body, "dve")

        def pe_z(pe, v):
            for j in range(8):
                s = v.place(j)
                pe.wait_ge(landed[s], v.landed(j))
                pe_slab_gemm(pe, v, j, s, {"cols": 256, "list": [(0, P, T2), (P, P, T2)]}, KD, lambda k: H[:, k, :], T2, 2 * j)
            v.end(U_Z)
            pe.drain().then_inc(pe_stage_end, 1)
            pe.wait_ge(act_stage_end, v.stages)
            pe.wait_ge(dve_stage_end, v.stages)

        def act_z(act, v):
            for n in range(16):
                act.wait_ge(filled[n % 8], v.filled(n % 8, n // 8))
                nc.scalar.activation(QK[:, n, :], ps[:, n % 8, :], ACT.Silu).then_inc(freed[n % 8], 1)
            v.end(U_Z)
            act.drain().then_inc(act_stage_end, 1)
            act.wait_ge(pe_stage_end, v.stages)
            act.wait_ge(dve_stage_end, v.stages)

        def act_read(act, v):
            for h in range(16):
                if h >= 2:
                    act.wait_ge(sems["sq"], v.of("sq", h - 1))
                nc.scalar.activation(VV[:, h % 2, :], OO[:, h, :], ACT.Square).then_inc(sems["squares"], 1)
            act.wait_ge(sems["scales"], v.of("scales", 1))
            nc.scalar.activation(MS[:, 0:64], MS[:, 0:64], ACT.Sqrt).then_inc(sems["scales"], 1)
            v.end(U_READ)
            act.drain().then_inc(act_stage_end, 1)
            act.wait_ge(pe_stage_end, v.stages)
            act.wait_ge(dve_stage_end, v.stages)

        def dve_read(dve, v):
            for h in range(16):
                dve.wait_ge(sems["squares"], v.of("squares", h + 1))
                nc.vector.tensor_reduce(MS[:, 4 * h:4 * h + 4], VV[:, h % 2, :].rearrange("p (t n) -> p t n", t=NT), AX.X, ALU.add).then_inc(sems["sq"], 1)
            dve.wait_ge(sems["sq"], v.of("sq", 16))
            nc.vector.tensor_scalar(MS[:, 0:64], MS[:, 0:64], 1.0 / P, EPS, ALU.mult, ALU.add).then_inc(sems["scales"], 1)
            dve.wait_ge(sems["scales"], v.of("scales", 2))
            nc.vector.reciprocal(MS[:, 0:64], MS[:, 0:64]).then_inc(dve_step, v.step())
            dve.wait_ge(dve_step, v.steps())
            for h in range(16):
                o = OO[:, h, :].rearrange("p (t n) -> p t n", t=NT)
                r = MS[:, 4 * h:4 * h + 4].rearrange("p (t n) -> p t n", n=1).broadcast_to([P, NT, P])
                nc.vector.tensor_tensor(o, o, r, ALU.mult).then_inc(sems["scaled"], 1)
            for h in range(16):
                dve.wait_ge(filled[h % 8], v.filled(h % 8, h // 8))
                nc.vector.scalar_tensor_tensor(VV[:, h, :], ps[:, h % 8, :], vec("dng"), QK[:, h, :], ALU.mult, ALU.mult).then_inc(freed[h % 8], 1)
            v.end(U_READ)
            dve.drain().then_inc(dve_stage_end, 1)
            dve.wait_ge(pe_stage_end, v.stages)
            dve.wait_ge(act_stage_end, v.stages)

        def pe_read(pe, v):
            for h in range(16):
                pe.wait_ge(sems["scaled"], v.of("scaled", h + 1))
                pe.wait_ge(freed[h % 8], v.free(h % 8, h // 8))
                for t in range(NT):
                    ins = nc.tensor.transpose(ps[:, h % 8, t * P:(t + 1) * P], OO[:, h, t * P:(t + 1) * P], ident[:])
                ins.then_inc(filled[h % 8], 1)
            v.end(U_READ)
            pe.drain().then_inc(pe_stage_end, 1)
            pe.wait_ge(act_stage_end, v.stages)
            pe.wait_ge(dve_stage_end, v.stages)

        def pe_dout(pe, v):
            for j in range(4):
                for t in range(2):
                    pe.wait_ge(freed[2 * j + t], v.free(2 * j + t))
                for kc in range(2):
                    s = v.place(2 * j + kc)
                    pe.wait_ge(landed[s], v.landed(2 * j + kc))
                    w = slab_view(s, KD, 256)
                    for t in range(2):
                        for k in range(KD):
                            ins = nc.tensor.matmul(ps[:, 2 * j + t, :], w[:, k, t * P:(t + 1) * P], VV[:, kc * KD + k, :],
                                                   start=(kc == 0 and k == 0), stop=(kc == 1 and k == KD - 1))
                            if t == 0 and k == 0:
                                ins.then_inc(sems["slab_begun"], 1)
                        if kc == 1:
                            ins.then_inc(filled[2 * j + t], 1)
            v.end(U_DOUT)
            pe.drain().then_inc(pe_stage_end, 1)
            pe.wait_ge(act_stage_end, v.stages)
            pe.wait_ge(dve_stage_end, v.stages)

        def gla_tiles():
            out = []
            for j in range(2):
                out += [(j, "q", 2 * j), (j, "q", 2 * j + 1)]
            for j in range(2):
                out += [(2 + j, "k", 2 * j), (2 + j, "k", 2 * j + 1)] + [(2 + j, "kt", (t, j)) for t in range(NT)]
            for j in range(4):
                out += [(4 + j, "vt", (t, j)) for t in range(NT)]
            for j in range(4):
                out += [(8 + j, "z", 2 * j), (8 + j, "z", 2 * j + 1)]
            out += [(12, "low", 0)]
            return out

        GTILES = gla_tiles()
        U_GIN = {**banks(len(GTILES)), "slab": 13}
        U_GLOG = {**banks(8), "abs": 8, "root": 8}

        def on_act(n, kind):
            return kind == "z" or (n % 2 == 0 and kind != "low")

        def pe_gin(pe, v):
            done = -1
            for n, (j, kind, x) in enumerate(GTILES):
                b = n % 8
                if j != done:
                    s = v.place(j)
                    pe.wait_ge(landed[s], v.landed(j))
                    w = slab_view(s, KD, 256)
                pe.wait_ge(freed[b], v.free(b, n // 8))
                for k in range(KD):
                    if kind in ("q", "k", "z"):
                        t = x % 2
                        ins = nc.tensor.matmul(ps[:, b, 0:L], w[:, k, t * P:(t + 1) * P], H[:, k, 0:L], start=(k == 0), stop=(k == KD - 1))
                    elif kind == "low":
                        ins = nc.tensor.matmul(ps[0:64, b, :], w[:, k, 0:64], H[:, k, :], start=(k == 0), stop=(k == KD - 1))
                    else:
                        t = x[0]
                        ins = nc.tensor.matmul(ps[:, b, 0:256], H[:, k, t * P:(t + 1) * P], w[:, k, :], start=(k == 0), stop=(k == KD - 1))
                    if j != done:
                        ins.then_inc(sems["slab_begun"], 1)
                        done = j
                ins.then_inc(filled[b], 1)
            v.end(U_GIN)
            pe.drain().then_inc(pe_stage_end, 1)
            pe.wait_ge(act_stage_end, v.stages)
            pe.wait_ge(dve_stage_end, v.stages)

        def gin_out(kind, x):
            if kind == "q":
                return QF[:, x, :]
            if kind == "k":
                return KF[:, x, :]
            if kind == "kt":
                return KTK[:, x[0], x[1] * 256:(x[1] + 1) * 256]
            if kind == "vt":
                return VTK[:, x[0], x[1] * 256:(x[1] + 1) * 256]
            return GZA[:, x, :]

        GZA = part(13312, KD, L)

        def act_gin(act, v):
            for n, (j, kind, x) in enumerate(GTILES):
                if on_act(n, kind):
                    b = n % 8
                    act.wait_ge(filled[b], v.filled(b, n // 8))
                    nc.scalar.activation(gin_out(kind, x), ps[:, b, 0:256], ACT.Silu if kind == "z" else ACT.Copy,
                                                 scale=float(P) ** -0.5 if kind == "q" else 1.0).then_inc(freed[b], 1)
            v.end(U_GIN)
            act.drain().then_inc(act_stage_end, 1)
            act.wait_ge(pe_stage_end, v.stages)
            act.wait_ge(dve_stage_end, v.stages)

        def dve_gin(dve, v):
            for n, (j, kind, x) in enumerate(GTILES):
                if on_act(n, kind):
                    continue
                b = n % 8
                dve.wait_ge(filled[b], v.filled(b, n // 8))
                if kind == "low":
                    ins = nc.vector.tensor_copy(LOW[0:64, :], ps[0:64, b, :])
                elif kind == "q":
                    ins = nc.vector.tensor_scalar(gin_out(kind, x), ps[:, b, 0:256], float(P) ** -0.5, None, ALU.mult)
                else:
                    ins = nc.vector.tensor_copy(gin_out(kind, x), ps[:, b, 0:256])
                ins.then_inc(freed[b], 1)
            v.end(U_GIN)
            dve.drain().then_inc(dve_stage_end, 1)
            dve.wait_ge(pe_stage_end, v.stages)
            dve.wait_ge(act_stage_end, v.stages)

        def pe_glog(pe, v):
            for n in range(8):
                t, d = n // 2, n % 2
                pe.wait_ge(freed[n], v.free(n))
                nc.tensor.matmul(ps[:, n, :], LOW[32 * d:32 * d + 32, t * P:(t + 1) * P], GW[32 * d:32 * d + 32, 1024:1536],
                                         start=True, stop=True).then_inc(filled[n], 1)
            v.end(U_GLOG)
            pe.drain().then_inc(pe_stage_end, 1)
            pe.wait_ge(act_stage_end, v.stages)
            pe.wait_ge(dve_stage_end, v.stages)

        GTMP = part(15360, 2, 1024)

        def gtmp(n):
            return GTMP[:, (n // 2) % 2, (n % 2) * 512:(n % 2) * 512 + 512]

        def dve_glog(dve, v):
            for i in range(10):
                if i < 8:
                    t, d = i // 2, i % 2
                    g = GK[:, t, d * 512:(d + 1) * 512]
                    dve.wait_ge(filled[i], v.filled(i))
                    nc.vector.tensor_tensor(g, ps[:, i, :], GW[:, d * 512:(d + 1) * 512], ALU.add).then_inc(freed[i], 1)
                    dve.wait_ge(freed[i], v.freed(i))
                    nc.vector.scalar_tensor_tensor(gtmp(i), g, -1.0, g, ALU.mult, ALU.max).then_inc(sems["abs"], 1)
                if i >= 2:
                    n = i - 2
                    t, d = n // 2, n % 2
                    g = GK[:, t, d * 512:(d + 1) * 512]
                    dve.wait_ge(sems["root"], v.of("root", n + 1))
                    nc.vector.scalar_tensor_tensor(g, g, 0.0, gtmp(n), ALU.min, ALU.subtract)
            nc.vector.tensor_copy(GZ[:, :, :], GZA[:, :, :])
            v.end(U_GLOG)
            dve.drain().then_inc(dve_stage_end, 1)
            dve.wait_ge(pe_stage_end, v.stages)
            dve.wait_ge(act_stage_end, v.stages)

        def act_glog(act, v):
            for n in range(8):
                act.wait_ge(sems["abs"], v.of("abs", n + 1))
                nc.scalar.activation(gtmp(n), gtmp(n), ACT.Exp, scale=-1.0).then_inc(act_step, v.step())
                act.wait_ge(act_step, v.steps())
                nc.scalar.activation(gtmp(n), gtmp(n), ACT.Ln, bias=ones[:, 0:1]).then_inc(sems["root"], 1)
            v.end(U_GLOG)
            act.drain().then_inc(act_stage_end, 1)
            act.wait_ge(pe_stage_end, v.stages)
            act.wait_ge(dve_stage_end, v.stages)

        GORDER = [[2, 3, 0, 1], [3, 2, 1, 0]]

        def gla_step_uses(st):
            u = {}
            if st < 3:
                u.update({0: 2, 1: 1, 7: 1, "ktl": 1})
            if st >= 2:
                for b in (2, 3, 4, 5, 6):
                    u[b] = 4
                u.update({"qx": 4, "at": 4})
            return u

        def gk_of(t, d, h):
            return GK[:, t, d * 512 + h * P:d * 512 + (h + 1) * P]

        def pe_gstep(pe, v, d, st):
            t = GORDER[d][st]
            if st < 3:
                pe.wait_ge(freed[0], v.free(0))
                nc.tensor.matmul(ps[:, 0, :], cst("after", d * P, d * P + P), GK[:, t, d * 512:(d + 1) * 512], start=True, stop=True).then_inc(filled[0], 1)
                pe.wait_ge(freed[1], v.free(1))
                for h in range(GH):
                    ins = nc.tensor.matmul(ps[:, 1, h:h + 1], gk_of(t, d, h), ones[:, 0:1], start=True, stop=True)
                ins.then_inc(filled[1], 1)
            if st >= 2:
                at = CCOL["exps"][0] + d * 1024
                for i in range(GH + 1):
                    if i < GH:
                        for q in range(2):
                            pe.wait_ge(freed[2 + q], v.free(2 + q, i))
                            nc.tensor.matmul(ps[:, 2 + q, :], gk_of(t, d, i), C[:, at + q * 512:at + (q + 1) * 512], start=True, stop=True).then_inc(filled[2 + q], 1)
                    if i >= 1:
                        h = i - 1
                        pe.wait_ge(sems["qx"], v.of("qx", h + 1))
                        for q in range(2):
                            pe.wait_ge(freed[4 + q], v.free(4 + q, h))
                            for n in range(4 * q, 4 * q + 4):
                                c0 = (n % 4) * P
                                if n == 0:
                                    ins = nc.tensor.matmul(ps[:, 4, 0:P], KF[:, h, t * P:(t + 1) * P], QF[:, h, t * P:(t + 1) * P], start=True, stop=True)
                                else:
                                    ins = nc.tensor.matmul(ps[:, 4 + q, c0:c0 + P], KX[:, h % 2, n * P:(n + 1) * P], QX[:, h % 2, n * P:(n + 1) * P],
                                                           start=True, stop=True)
                            ins.then_inc(filled[4 + q], 1)
                        pe.wait_ge(sems["at"], v.of("at", h + 1))
                        pe.wait_ge(freed[6], v.free(6, h))
                        nc.tensor.matmul(ps[:, 6, 0:GV], ATG[:, h % 2, :], VTK[:, t, h * GV:(h + 1) * GV], start=True, stop=False)
                        nc.tensor.matmul(ps[:, 6, 0:GV], QX[:, h % 2, 0:P], SG[:, h, :], start=False, stop=True).then_inc(filled[6], 1)
            if st < 3:
                pe.wait_ge(sems["ktl"], v.of("ktl", 1))
                for q, b in ((0, 7), (1, 0)):
                    pe.wait_ge(freed[b], v.free(b, q))
                    for h in range(2 * q, 2 * q + 2):
                        ins = nc.tensor.matmul(ps[:, b, (h % 2) * GV:(h % 2 + 1) * GV], KTL[:, 0, h * P:(h + 1) * P], VTK[:, t, h * GV:(h + 1) * GV],
                                               start=True, stop=True)
                    ins.then_inc(filled[b], 1)
            v.end(gla_step_uses(st))
            pe.drain().then_inc(pe_stage_end, 1)
            pe.wait_ge(act_stage_end, v.stages)
            pe.wait_ge(dve_stage_end, v.stages)

        def act_gstep(act, v, d, st):
            if st < 3:
                act.wait_ge(filled[0], v.filled(0))
                nc.scalar.activation(KTL[:, 0, :], ps[:, 0, :], ACT.Exp, scale=1.0 / 16).then_inc(freed[0], 1)
                act.wait_ge(filled[1], v.filled(1))
                nc.scalar.activation(ETG[:, 0, :], ps[:, 1, 0:GH], ACT.Exp, scale=1.0 / 16).then_inc(freed[1], 1)
            if st >= 2:
                for h in range(GH):
                    if h >= 2:
                        act.wait_ge(sems["qx"], v.of("qx", h - 1))
                    for q in range(2):
                        act.wait_ge(filled[2 + q], v.filled(2 + q, h))
                        nc.scalar.activation(EX[:, h % 2, q * 512:(q + 1) * 512], ps[:, 2 + q, :], ACT.Exp, scale=1.0 / 16).then_inc(freed[2 + q], 1)
            v.end(gla_step_uses(st))
            act.drain().then_inc(act_stage_end, 1)
            act.wait_ge(pe_stage_end, v.stages)
            act.wait_ge(dve_stage_end, v.stages)

        def dve_gstep(dve, v, d, st):
            t = GORDER[d][st]
            if st < 3:
                dve.wait_ge(freed[0], v.freed(0))
                nc.vector.tensor_tensor(KTL[:, 0, :], KTL[:, 0, :], KTK[:, t, :], ALU.mult).then_inc(sems["ktl"], 1)
            if st >= 2:
                masks = cst("upper" if d == 0 else "lower", 0, 1024)
                for i in range(GH + 1):
                    if i < GH:
                        dve.wait_ge(freed[2], v.freed(2, i + 1))
                        dve.wait_ge(freed[3], v.freed(3, i + 1))
                        if i >= 2:
                            dve.wait_ge(filled[6], v.filled(6, i - 2))
                        e = EX[:, i % 2, :].rearrange("p (n t) -> p n t", t=P)
                        for dst, src in ((QX, QF), (KX, KF)):
                            x = src[:, i:i + 1, t * P:(t + 1) * P].broadcast_to([P, 8, P])
                            ins = nc.vector.tensor_tensor(dst[:, i % 2, :].rearrange("p (n t) -> p n t", t=P), e, x, ALU.mult)
                        ins.then_inc(sems["qx"], 1)
                    if i >= 1:
                        h = i - 1
                        for q in range(2):
                            dve.wait_ge(filled[4 + q], v.filled(4 + q, h))
                            nc.vector.tensor_tensor(AP_[:, h % 2, q * 512:(q + 1) * 512], ps[:, 4 + q, :], masks[:, q * 512:(q + 1) * 512], ALU.mult).then_inc(freed[4 + q], 1)
                        dve.wait_ge(freed[5], v.freed(5, h + 1))
                        if h >= 2:
                            dve.wait_ge(filled[6], v.filled(6, h - 2))
                        nc.vector.tensor_reduce(ATG[:, h % 2, :], AP_[:, h % 2, :].rearrange("p (n t) -> p t n", t=P), AX.X, ALU.add).then_inc(sems["at"], 1)
                        dve.wait_ge(filled[6], v.filled(6, h))
                        o = OG[:, t, h * GV:(h + 1) * GV]
                        if d == 0:
                            nc.vector.tensor_copy(o, ps[:, 6, 0:GV]).then_inc(freed[6], 1)
                        else:
                            nc.vector.tensor_tensor(o, ps[:, 6, 0:GV], o, ALU.add).then_inc(freed[6], 1)
            if st < 3:
                dve.wait_ge(freed[1], v.freed(1))
                for q, b in ((0, 7), (1, 0)):
                    dve.wait_ge(filled[b], v.filled(b, q))
                    for h in range(2 * q, 2 * q + 2):
                        dS = ps[:, b, (h % 2) * GV:(h % 2 + 1) * GV]
                        if st == 0:
                            ins = nc.vector.tensor_copy(SG[:, h, :], dS)
                        else:
                            ins = nc.vector.scalar_tensor_tensor(SG[:, h, :], SG[:, h, :], ETG[:, 0, h:h + 1], dS, ALU.mult, ALU.add)
                    ins.then_inc(freed[b], 1)
            v.end(gla_step_uses(st))
            dve.drain().then_inc(dve_stage_end, 1)
            dve.wait_ge(pe_stage_end, v.stages)
            dve.wait_ge(act_stage_end, v.stages)

        U_GREAD = {**banks(8), "sq": 2, "squares": 2, "abs": 1, "root": 1, "at": 1}

        def act_gread(act, v):
            for t in range(2):
                if t:
                    act.wait_ge(sems["sq"], v.of("sq", 1))
                nc.scalar.activation(GSQ[:, :], OG[:, t, :], ACT.Square).then_inc(sems["squares"], 1)
            act.wait_ge(sems["abs"], v.of("abs", 1))
            nc.scalar.activation(GMS[:, 0:8], GMS[:, 0:8], ACT.Sqrt).then_inc(sems["root"], 1)
            v.end(U_GREAD)
            act.drain().then_inc(act_stage_end, 1)
            act.wait_ge(pe_stage_end, v.stages)
            act.wait_ge(dve_stage_end, v.stages)

        def dve_gread(dve, v):
            for t in range(2):
                dve.wait_ge(sems["squares"], v.of("squares", t + 1))
                nc.vector.tensor_reduce(GMS[:, 4 * t:4 * t + 4], GSQ[:, :].rearrange("p (h n) -> p h n", h=GH), AX.X, ALU.add).then_inc(sems["sq"], 1)
            dve.wait_ge(sems["sq"], v.of("sq", 2))
            nc.vector.tensor_scalar(GMS[:, 0:8], GMS[:, 0:8], 1.0 / GV, EPS, ALU.mult, ALU.add).then_inc(sems["abs"], 1)
            dve.wait_ge(sems["root"], v.of("root", 1))
            nc.vector.reciprocal(GMS[:, 0:8], GMS[:, 0:8]).then_inc(dve_step, v.step())
            dve.wait_ge(dve_step, v.steps())
            for t in range(2):
                o = OG[:, t, :].rearrange("p (h n) -> p h n", h=GH)
                ins = nc.vector.tensor_tensor(o, o, GMS[:, 4 * t:4 * t + 4].rearrange("p (h n) -> p h n", n=1).broadcast_to([P, GH, GV]), ALU.mult)
            ins.then_inc(sems["at"], 1)
            for f in range(8):
                dve.wait_ge(filled[f], v.filled(f))
                nc.vector.scalar_tensor_tensor(GMIX[:, f, :], ps[:, f, 0:L], vec("glag", f % 2), GZ[:, f, :], ALU.mult, ALU.mult).then_inc(freed[f], 1)
            v.end(U_GREAD)
            dve.drain().then_inc(dve_stage_end, 1)
            dve.wait_ge(pe_stage_end, v.stages)
            dve.wait_ge(act_stage_end, v.stages)

        def pe_gread(pe, v):
            pe.wait_ge(sems["at"], v.of("at", 1))
            for f in range(8):
                pe.wait_ge(freed[f], v.free(f))
                for t in range(2):
                    ins = nc.tensor.transpose(ps[:, f, t * P:(t + 1) * P], OG[:, t, f * P:(f + 1) * P], ident[:])
                ins.then_inc(filled[f], 1)
            v.end(U_GREAD)
            pe.drain().then_inc(pe_stage_end, 1)
            pe.wait_ge(act_stage_end, v.stages)
            pe.wait_ge(dve_stage_end, v.stages)

        nslabs = A["w"].shape[0]

        @block.sync
        def _(sp):
            for s in range(RING):
                sp.dma_start(ring[:, s], A["w"][s]).then_inc(landed[s], 16)
            rounds, rest = (nslabs - RING) // RING, (nslabs - RING) % RING
            with sp.Fori(0, rounds) as i:
                for s in range(RING):
                    sp.wait_ge(sems["slab_begun"], i * RING + (s + 2))
                    sp.dma_start(ring[:, s], A["w"][i * RING + (s + RING)]).then_inc(landed[s], 16)
            for s in range(rest):
                n = RING + rounds * RING + s
                sp.wait_ge(sems["slab_begun"], n - RING + 2)
                sp.dma_start(ring[:, s], A["w"][n]).then_inc(landed[s], 16)
            sp.wait_ge(sems["prepared"], 1)
            sp.dma_start(out, X[:, :, 0:out.shape[2]]).then_inc(sems["stored"], 16)
            sp.wait_ge(sems["stored"], 16)

        spill = nc.dram_tensor("x_spill", [P, KD, T2], F32, kind="Internal").ap()

        def first_uses(l):
            return [U_MOD, U_NORM, U_IN, U_LORA, U_UP, u_attn(l), u_fnet(l), u_filter(l), u_hyena(l), U_OUT, U_NORM, U_MLP]

        @block.gpsimd
        def _(pool):
            nc.gpsimd.memset(ones[:], 1.0).then_inc(pool_step, 1)
            nc.gpsimd.memset(ident[:], 0.0).then_inc(pool_step, 1)
            pool.wait_ge(pool_step, 2)
            nc.gpsimd.affine_select(out=ident[:], in_=ident[:], compare_op=ALU.not_equal, fill=1.0, base=0,
                                    pattern=[[-1, P]], channel_multiplier=1).then_inc(sems["first_loaded"], 16)
            v = View("pool")
            v.pass_over({})
            for l in range(DEPTH):
                for uses in first_uses(l):
                    v.pass_over(uses)
            v.pass_over(U_FNORM)
            for uses in [{}, U_MOD, U_NORM]:
                v.pass_over(uses)
            for n, k in U_CONV_BODY.items():
                v.base[n] = v.base.get(n, 0) + 3 * k
            for uses in [{**U_CONV_BODY, "gates": 1}, U_L2, U_VT, U_GATES]:
                v.pass_over(uses)
            pool_delta(pool, v)

        @block.scalar
        def _(act):
            v = View("act")
            act.dma_start(V[:], A["vecs"]).then_inc(sems["first_loaded"], 16)
            act.dma_start(X[:], A["x1"]).then_inc(sems["loaded"], 16)
            act.dma_start(C[:], A["first"]).then_inc(sems["loaded"], 16)
            act.dma_start(HYW[:], A["hyw"]).then_inc(sems["loaded"], 16)
            act.wait_ge(sems["first_loaded"], 32)
            for blk in range(2):
                nc.scalar.activation(cs[:, blk, :], vec(f"c{blk + 1}", 0, 16), ACT.Silu)
            v.end({})
            act.drain().then_inc(act_stage_end, 1)
            act.wait_ge(pe_stage_end, v.stages)
            act.wait_ge(dve_stage_end, v.stages)
            for l in range(DEPTH):
                T = T2 if l == 0 else L
                act_mod(act, v, 48 if l == 0 else 0)
                act_norm(act, v, 0, T2, 0)
                act_in(act, v, l)
                act_lora(act, v, l)
                act_up(act, v, l)
                act_attn(act, v, l)
                act_fnet(act, v, l)
                act_filter(act, v, l)
                act_hyena(act, v, l)
                v.end(U_OUT)
                act.drain().then_inc(act_stage_end, 1)
                act.wait_ge(pe_stage_end, v.stages)
                act.wait_ge(dve_stage_end, v.stages)
                act_norm(act, v, 1, T, 3 * KD)
                act_mlp(act, v, T)
            act_norm(act, v, 0, L, 0, plain=True)
            act.dma_start(C[:, 0:NCST2], A["second"]).then_inc(sems["second_loaded"], 16)
            act.dma_start(X[:, :, L:T2], A["ctx2"]).then_inc(sems["second_loaded"], 16)
            act.wait_ge(sems["second_loaded"], 32)
            v.end({})
            act.drain().then_inc(act_stage_end, 1)
            act.wait_ge(pe_stage_end, v.stages)
            act.wait_ge(dve_stage_end, v.stages)
            act_mod(act, v)
            act_norm(act, v, 0, T2, 0)
            act.dma_start(spill, X[:]).then_inc(sems["spilled"], 16)
            act_conv(act, v)
            act_l2(act, v)
            act_vt(act, v)
            act.wait_ge(sems["spilled"], 16)
            act_gates(act, v)
            act_delta(act, v)
            act.dma_start(X[:], spill).then_inc(sems["restored"], 16)
            act.wait_ge(sems["restored"], 16)
            v.end({})
            act.drain().then_inc(act_stage_end, 1)
            act.wait_ge(pe_stage_end, v.stages)
            act.wait_ge(dve_stage_end, v.stages)
            act_norm(act, v, 0, T2, 0)
            act_z(act, v)
            act_read(act, v)
            v.end(U_DOUT)
            act.drain().then_inc(act_stage_end, 1)
            act.wait_ge(pe_stage_end, v.stages)
            act.wait_ge(dve_stage_end, v.stages)
            act_norm(act, v, 1, T2, 3 * KD)
            act_mlp(act, v, T2)
            act.dma_start(GW[:], A["gla"]).then_inc(sems["second_loaded"], 16)
            act_mod(act, v)
            act_norm(act, v, 0, T2, 0)
            act_gin(act, v)
            act.wait_ge(sems["second_loaded"], 48)
            v.end({})
            act.drain().then_inc(act_stage_end, 1)
            act.wait_ge(pe_stage_end, v.stages)
            act.wait_ge(dve_stage_end, v.stages)
            act_glog(act, v)
            for d in DIRS:
                for st in range(4):
                    act_gstep(act, v, d, st)
            act_gread(act, v)
            v.end(U_OUT)
            act.drain().then_inc(act_stage_end, 1)
            act.wait_ge(pe_stage_end, v.stages)
            act.wait_ge(dve_stage_end, v.stages)
            act_norm(act, v, 1, L, 3 * KD)
            act_mlp(act, v, L)

        @block.tensor
        def _(pe):
            v = View("pe")
            v.end({})
            pe.drain().then_inc(pe_stage_end, 1)
            pe.wait_ge(act_stage_end, v.stages)
            pe.wait_ge(dve_stage_end, v.stages)
            for l in range(DEPTH):
                T = T2 if l == 0 else L
                pe_mod(pe, v, 0)
                pe_norm(pe, v, T2)
                pe_in(pe, v, l)
                pe_lora(pe, v, l)
                pe_up(pe, v, l)
                pe_attn(pe, v, l)
                pe_fnet(pe, v, l)
                pe_filter(pe, v, l)
                pe_hyena(pe, v, l)
                pe_out(pe, v, T, MIX)
                pe_norm(pe, v, T)
                pe_mlp(pe, v, T)
            pe_final(pe, v)
            v.end({})
            pe.drain().then_inc(pe_stage_end, 1)
            pe.wait_ge(act_stage_end, v.stages)
            pe.wait_ge(dve_stage_end, v.stages)
            pe_mod(pe, v, 1)
            pe_norm(pe, v, T2)
            pe_conv(pe, v)
            pe_l2(pe, v)
            pe_vt(pe, v)
            pe_gates(pe, v)
            pe_delta(pe, v)
            v.end({})
            pe.drain().then_inc(pe_stage_end, 1)
            pe.wait_ge(act_stage_end, v.stages)
            pe.wait_ge(dve_stage_end, v.stages)
            pe_norm(pe, v, T2)
            pe_z(pe, v)
            pe_read(pe, v)
            pe_dout(pe, v)
            pe_norm(pe, v, T2)
            pe_mlp(pe, v, T2)
            pe_mod(pe, v, 1)
            pe_norm(pe, v, T2)
            pe_gin(pe, v)
            v.end({})
            pe.drain().then_inc(pe_stage_end, 1)
            pe.wait_ge(act_stage_end, v.stages)
            pe.wait_ge(dve_stage_end, v.stages)
            pe_glog(pe, v)
            for d in DIRS:
                for st in range(4):
                    pe_gstep(pe, v, d, st)
            pe_gread(pe, v)
            pe_out(pe, v, L, GMIX)
            pe_norm(pe, v, L)
            pe_mlp(pe, v, L)

        @block.vector
        def _(dve):
            v = View("dve")
            for b in range(8):
                nc.vector.memset(RK[:, b:b + 1], 0.0).then_inc(freed[b], 1)
            v.end({})
            dve.drain().then_inc(dve_stage_end, 1)
            dve.wait_ge(pe_stage_end, v.stages)
            dve.wait_ge(act_stage_end, v.stages)
            for l in range(DEPTH):
                T = T2 if l == 0 else L
                dve_mod(dve, v, l, "b_mod", "g1", "g2")
                dve_norm(dve, v, T2)
                dve_in(dve, v, l)
                dve_lora(dve, v, l)
                dve_up(dve, v, l)
                dve_attn(dve, v, l)
                dve_fnet(dve, v, l)
                dve_filter(dve, v, l)
                dve_hyena(dve, v, l)
                dve_out(dve, v, T, U_OUT)
                dve_norm(dve, v, T)
                dve_mlp(dve, v, T)
            dve_final(dve, v)
            v.end({})
            dve.drain().then_inc(dve_stage_end, 1)
            dve.wait_ge(pe_stage_end, v.stages)
            dve.wait_ge(act_stage_end, v.stages)
            dve_mod(dve, v, 0, "b_ada", "gm", "gn")
            dve_norm(dve, v, T2)
            dve_conv(dve, v)
            dve_l2(dve, v)
            dve_vt(dve, v)
            dve_gates(dve, v)
            dve_delta(dve, v)
            v.end({})
            dve.drain().then_inc(dve_stage_end, 1)
            dve.wait_ge(pe_stage_end, v.stages)
            dve.wait_ge(act_stage_end, v.stages)
            dve_norm(dve, v, T2)
            v.end(U_Z)
            dve.drain().then_inc(dve_stage_end, 1)
            dve.wait_ge(pe_stage_end, v.stages)
            dve.wait_ge(act_stage_end, v.stages)
            dve_read(dve, v)
            dve_out(dve, v, T2, U_DOUT)
            dve_norm(dve, v, T2)
            dve_mlp(dve, v, T2)
            dve_mod(dve, v, 1, "b_ada", "gm", "gn")
            dve_norm(dve, v, T2)
            dve_gin(dve, v)
            v.end({})
            dve.drain().then_inc(dve_stage_end, 1)
            dve.wait_ge(pe_stage_end, v.stages)
            dve.wait_ge(act_stage_end, v.stages)
            dve_glog(dve, v)
            for d in DIRS:
                for st in range(4):
                    dve_gstep(dve, v, d, st)
            dve_gread(dve, v)
            dve_out(dve, v, L, U_OUT)
            dve_norm(dve, v, L)
            dve_mlp(dve, v, L)
            nc.vector.memset(MS[:, 0:1], 0.0).then_inc(sems["prepared"], 1)


def feature_tiles(a, axis_tokens=True):
    t, f = a.shape
    return np.ascontiguousarray(a.T.reshape(f // P, P, t).transpose(1, 0, 2))


def vector_columns(a, twice=False):
    a = np.asarray(a)
    c = a.reshape(-1, P).T
    return np.repeat(c, 2, axis=1) if twice else c


def slabs_of(w, cols=256, rows=1024):
    K, N = w.shape
    out = []
    for c in range(0, N, cols):
        for r in range(0, K, rows):
            blk = w[r:r + rows, c:c + cols]
            k, n = blk.shape
            blk = blk.reshape(k // P, P, n).transpose(1, 0, 2)
            if n < cols:
                blk = np.concatenate([blk, np.zeros((P, k // P, cols - n), w.dtype)], 2)
            blk = blk.reshape(P, -1)
            if blk.shape[1] < SLAB:
                blk = np.concatenate([blk, np.zeros((P, SLAB - blk.shape[1]), w.dtype)], 1)
            out.append(blk)
    return out


def mlp_slabs(w1, w2):
    out = []
    for q in range(0, HT * P, D):
        out += slabs_of(w1[:, q:q + D]) + slabs_of(w2[q:q + D])
    return out


PARTNER = np.array([a * 16 + (j + 8) % 16 for a in range(2) for j in range(16)])


def first_slabs(I, l):
    z = np.zeros
    w = I["w_in"][l]
    kr = w[:, OFF_KR:OFF_F]
    kr_tile = np.concatenate([z((D, 64), np.float32), kr, kr[:, PARTNER]], 1)
    w_in = np.concatenate([w[:, :OFF_KV], kr_tile, w[:, OFF_KV:OFF_KR], w[:, OFF_F:]], 1)
    uq = I["w_uq"][l].reshape(QLORA, HEADS, NOPE + ROPE)
    uq = np.concatenate([uq, uq[:, :, NOPE:][:, :, PARTNER]], 2).reshape(QLORA, HEADS * P)
    ukv = I["w_ukv"][l].reshape(KVLORA, HEADS, NOPE + VH)
    uk = ukv[:, :, :NOPE].reshape(KVLORA, -1)
    uv = ukv[:, :, NOPE:].reshape(KVLORA, -1)
    tile = lambda m: m.reshape(2, P, -1).transpose(1, 0, 2).reshape(P, -1)
    out = slabs_of(I["w_mod"][l]) + slabs_of(w_in) + slabs_of(uq, 512) + [np.concatenate([tile(uk), tile(uv)], 1)]
    return out + slabs_of(I["w_out"][l]) + mlp_slabs(I["w_mlp1"][l], I["w_mlp2"][l])


def second_slabs(I):
    w = I["dn_w_in_2"][0]
    out = slabs_of(I["ada_w_2"][0]) + slabs_of(w[:, :4096]) + slabs_of(w[:, 6144:]) + slabs_of(w[:, 4096:6144])
    out += slabs_of(I["dn_w_out_2"][0]) + mlp_slabs(I["ffn_w1_2"][0], I["ffn_w2_2"][0])
    g = I["gla_w_in_2"][0]
    z = np.zeros((D, 16), np.float32)
    low = np.concatenate([g[:, 3072:3088], z, g[:, 3088:3104], z], 1)
    out += slabs_of(I["ada_w_2"][1]) + slabs_of(g[:, :3072]) + slabs_of(low)
    return out + slabs_of(I["gla_w_out_2"][0]) + mlp_slabs(I["ffn_w1_2"][1], I["ffn_w2_2"][1])


def arrays(I):
    I = {n: np.asarray(a) for n, a in I.items()}
    vc = vector_columns
    pad = lambda a: np.concatenate([a, np.zeros((P - a.shape[0], a.shape[1]), np.float32)], 0)
    pair = lambda a, b: np.stack([vc(a), vc(b)], 2).reshape(P, -1)
    parts = {
        "c1": pair(I["c"], I["c_ctx"]), "c2": pair(I["c_2"], I["c_ctx_2"]),
        "g1": vc(I["norm1_g"], True), "g2": vc(I["norm2_g"], True), "b_mod": vc(I["b_mod"], True),
        "qg": vc(I["q_norm_g"]), "kvg": vc(I["kv_norm_g"]), "cw": vc(I["hy_conv_w"]), "cb": vc(I["hy_conv_b"]),
        "hyd": vc(I["hy_d"]), "gf": vc(I["final_norm_g"]), "b_ada": vc(I["ada_b_2"], True),
        "gm": vc(I["norm_mix_g_2"], True), "gn": vc(I["norm_ffn_g_2"], True),
        "hb1": pad(I["hy_b1"].T), "hfreq": pad(I["hy_freq"].T), "hb2": pad(I["hy_b2"].T),
        "dncw": I["dn_conv_w_2"][0].reshape(32, P, 5).transpose(1, 0, 2).reshape(P, -1),
        "dng": vc(I["dn_norm_g_2"]), "glag": vc(I["gla_norm_g_2"]),
    }
    parts["dt"] = np.broadcast_to(I["dn_dt_bias_2"][0].reshape(1, 32), (P, 32))
    parts["alog"] = np.broadcast_to(I["dn_a_log_2"][0].reshape(1, 32), (P, 32))
    vecs = np.concatenate([parts[n] for n, _ in VECS], 1)
    g2 = I["gla_gate_w2_2"][0]
    gz = np.zeros((16, 512), np.float32)
    gw = np.concatenate([g2[0], gz, g2[1], gz, np.zeros((64, 512), np.float32)], 0)
    gla = np.concatenate([np.broadcast_to(I["gla_gate_b2_2"][0].reshape(1, 1024), (P, 1024)), gw], 1)
    cst2 = second_constants()
    hyw = np.stack([np.concatenate([pad(I["hy_w1"][l]), pad(I["hy_w2"][l]), pad(I["hy_w3"][l])], 1) for l in range(DEPTH)], 1)
    cst = first_constants()
    slabs = first_slabs(I, 0) + first_slabs(I, 1) + second_slabs(I)
    return {
        "w": np.stack(slabs), "vecs": vecs, "hyw": hyw,
        "x1": np.concatenate([feature_tiles(I["x"][0]), feature_tiles(I["ctx"][0])], 2),
        "ctx2": feature_tiles(I["ctx_2"][0]), "gla": gla,
        "second": np.concatenate([cst2[n] for n, _ in SECOND], 1),
        "first": np.concatenate([cst[n] for n, _ in FIRST], 1),
    }


def kernel(**inputs):
    import concourse.bacc as bacc
    from concourse.bass_utils import run_bass_kernel_spmd

    nc = bacc.Bacc("TRN2", target_bir_lowering=False, num_devices=1)
    laid_out = arrays(inputs)
    sent = {f"in_{n}_dram": np.ascontiguousarray(a) for n, a in laid_out.items()}
    A = {n: nc.dram_tensor(f"in_{n}_dram", a.shape, F32, kind="ExternalInput").ap() for n, a in laid_out.items()}
    out = nc.dram_tensor("out_0_dram", (P, KD, L), F32, kind="ExternalOutput").ap()
    build(nc, A, out)
    got = run_bass_kernel_spmd(nc, [sent], core_ids=[0]).results[0]["out_0_dram"]
    return np.ascontiguousarray(got.transpose(1, 0, 2).reshape(D, L).T[None])
```
